# Optimizing a Trainium2 kernel written in Bass

```python
import jax, jax.numpy as jnp
from jax import lax
import numpy as np

D_MODEL = 1024
BATCH = 1
SEQ = 256
DEPTH = 2

HEAD_DIM = 64
D_MIX = D_MODEL
NSA_HEADS = (D_MIX // 2) // HEAD_DIM
NSA_KV_HEADS = 2
NSA_GROUP = NSA_HEADS // NSA_KV_HEADS
CMP_LEN = 32
CMP_STRIDE = 16
CMP_HIDDEN = 256
SLC_BLOCK = 64
SLC_TOPK = 16
WINDOW = 512
WIN_BLOCK = 128
SEL_QBLOCK = 64
N_BRANCH = 3
CONV_CH = D_MIX // 4
CONV_K = 31
RET_HEADS = (D_MIX // 4) // HEAD_DIM
RET_CHUNK = 128
ROPE_BASE = 10000.0
D_FF = ((8 * D_MODEL // 3 + 255) // 256) * 256
N_EXPERTS = 8
TOP_K = 2
MOE_BLOCK = 256
NSA_Q_W = NSA_HEADS * HEAD_DIM
NSA_KV_W = NSA_KV_HEADS * HEAD_DIM
NSA_GATE_W = NSA_HEADS * N_BRANCH
RET_W = RET_HEADS * HEAD_DIM
IN_SPLITS = (NSA_Q_W, NSA_KV_W, NSA_KV_W, NSA_KV_W, NSA_KV_W, NSA_KV_W, NSA_KV_W, NSA_GATE_W, 2 * CONV_CH, RET_W, RET_W, RET_W, RET_W)
D_IN = NSA_Q_W + 6 * NSA_KV_W + NSA_GATE_W + 2 * CONV_CH + 4 * RET_W
NEG_INF = -1e30
FORCE_SCORE = 1e9
EPS = 1e-6

kernel_name = 'hybrid_nsa_conformer_retention_moe'

def rmsnorm(x, g):
    xf = x.astype(jnp.float32)
    xf = xf * lax.rsqrt(jnp.mean(xf * xf, axis=-1, keepdims=True) + EPS)
    return (xf * g.astype(jnp.float32)).astype(x.dtype)

def masked_softmax(s, mask):
    s = jnp.where(mask, s.astype(jnp.float32), NEG_INF)
    p = jax.nn.softmax(s, axis=-1)
    return jnp.where(mask, p, 0.0)

def compress_blocks(kv, pe, w1, w2):
    B, T, G, hd = kv.shape
    r = CMP_LEN // CMP_STRIDE
    ns = T // CMP_STRIDE
    sub = kv.reshape(B, ns, CMP_STRIDE, G, hd)
    blocks = jnp.concatenate([sub[:, j:ns - r + 1 + j] for j in range(r)], axis=2)
    blocks = blocks + pe[None, None, :, None, :]
    nc = blocks.shape[1]
    flat = blocks.transpose(0, 1, 3, 2, 4).reshape(B, nc, G, CMP_LEN * hd)
    return jax.nn.silu(flat @ w1) @ w2

def nsa_mixer(q, k_c, v_c, k_s, v_s, k_w, v_w, gate_logits, cmp_pe, cmp_w1, cmp_w2):
    B, T, _ = q.shape
    G, HPG, hd = NSA_KV_HEADS, NSA_GROUP, HEAD_DIM
    scale = hd ** -0.5
    q5 = q.reshape(B, T, G, HPG, hd)
    kv4 = lambda a: a.reshape(B, T, G, hd)
    k_c, v_c, k_s, v_s, k_w, v_w = map(kv4, (k_c, v_c, k_s, v_s, k_w, v_w))
    t_pos = jnp.arange(T)

    kc = compress_blocks(k_c, cmp_pe[0], cmp_w1[0], cmp_w2[0])
    vc = compress_blocks(v_c, cmp_pe[1], cmp_w1[1], cmp_w2[1])
    nc = kc.shape[1]
    cmp_start = jnp.arange(nc) * CMP_STRIDE
    cmp_mask = (cmp_start + CMP_LEN - 1)[None, :] <= t_pos[:, None]
    s_cmp = jnp.einsum('btghd,bcgd->bghtc', q5, kc) * scale
    p_cmp = masked_softmax(s_cmp, cmp_mask[None, None, None])
    o_cmp = jnp.einsum('bghtc,bcgd->btghd', p_cmp, vc.astype(jnp.float32))

    ns = T // SLC_BLOCK
    slc_start = jnp.arange(ns) * SLC_BLOCK
    overlap = ((cmp_start[:, None] < slc_start[None, :] + SLC_BLOCK) &
               (cmp_start[:, None] + CMP_LEN > slc_start[None, :])).astype(jnp.float32)
    imp = jnp.einsum('bgtc,cs->bgts', p_cmp.sum(axis=2), overlap)
    cur = t_pos // SLC_BLOCK
    j = jnp.arange(ns)
    valid = j[None, :] <= cur[:, None]
    forced = (j[None, :] == 0) | (j[None, :] == cur[:, None]) | (j[None, :] == cur[:, None] - 1)
    imp = jnp.where(valid, jnp.where(forced, FORCE_SCORE, imp), NEG_INF)
    k_top = min(SLC_TOPK, ns)
    _, idx = lax.top_k(imp, k_top)

    ks_blocks = k_s.reshape(B, ns, SLC_BLOCK, G, hd).transpose(0, 3, 1, 2, 4)
    vs_blocks = v_s.reshape(B, ns, SLC_BLOCK, G, hd).transpose(0, 3, 1, 2, 4)
    nq = T // SEL_QBLOCK
    q_ch = q5.reshape(B, nq, SEL_QBLOCK, G, HPG, hd).transpose(1, 0, 3, 2, 4, 5)
    idx_ch = idx.reshape(B, G, nq, SEL_QBLOCK, k_top).transpose(2, 0, 1, 3, 4)
    t_ch = t_pos.reshape(nq, SEL_QBLOCK)
    gather = jax.vmap(jax.vmap(lambda blk, ix: blk[ix]))
    n_sel = k_top * SLC_BLOCK

    def sel_block(args):
        qb, ib, tb = args
        kg = gather(ks_blocks, ib).reshape(B, G, SEL_QBLOCK, n_sel, hd)
        vg = gather(vs_blocks, ib).reshape(B, G, SEL_QBLOCK, n_sel, hd)
        kpos = (ib[..., None] * SLC_BLOCK + jnp.arange(SLC_BLOCK)).reshape(B, G, SEL_QBLOCK, n_sel)
        mask = kpos <= tb[None, None, :, None]
        s = jnp.einsum('bgqhd,bgqnd->bgqhn', qb, kg) * scale
        p = masked_softmax(s, mask[:, :, :, None, :])
        return jnp.einsum('bgqhn,bgqnd->bgqhd', p, vg.astype(jnp.float32))

    o_sel = lax.map(sel_block, (q_ch, idx_ch, t_ch))
    o_sel = o_sel.transpose(1, 0, 3, 2, 4, 5).reshape(B, T, G, HPG, hd)

    nb = T // WIN_BLOCK
    nwb = WINDOW // WIN_BLOCK
    qb = q5.reshape(B, nb, WIN_BLOCK, G, HPG, hd)
    def band(a):
        a = a.reshape(B, nb, WIN_BLOCK, G, hd)
        a = jnp.pad(a, ((0, 0), (nwb, 0), (0, 0), (0, 0), (0, 0)))
        return jnp.concatenate([a[:, j:j + nb] for j in range(nwb + 1)], axis=2)
    kwin, vwin = band(k_w), band(v_w)
    qpos = jnp.arange(nb)[:, None] * WIN_BLOCK + jnp.arange(WIN_BLOCK)[None, :]
    kpos = (jnp.arange(nb)[:, None] - nwb) * WIN_BLOCK + jnp.arange((nwb + 1) * WIN_BLOCK)[None, :]
    dpos = qpos[:, :, None] - kpos[:, None, :]
    wmask = (dpos >= 0) & (dpos < WINDOW) & (kpos[:, None, :] >= 0)
    s_w = jnp.einsum('bnqghd,bnkgd->bnghqk', qb, kwin) * scale
    p_w = masked_softmax(s_w, wmask[None, :, None, None])
    o_win = jnp.einsum('bnghqk,bnkgd->bnqghd', p_w, vwin.astype(jnp.float32)).reshape(B, T, G, HPG, hd)

    g = jax.nn.sigmoid(gate_logits.astype(jnp.float32)).reshape(B, T, G, HPG, N_BRANCH)
    o = g[..., 0:1] * o_cmp + g[..., 1:2] * o_sel + g[..., 2:3] * o_win
    return o.reshape(B, T, NSA_Q_W).astype(q.dtype)

def conformer_conv(u, conv_w, conv_b, ln_g, ln_b, conv_pw):
    a, gt = jnp.split(u, 2, axis=-1)
    h = a * jax.nn.sigmoid(gt)
    h = lax.conv_general_dilated(h, conv_w[:, None, :].astype(h.dtype), window_strides=(1,),
                                 padding=[(CONV_K - 1, 0)], dimension_numbers=('NWC', 'WIO', 'NWC'),
                                 feature_group_count=CONV_CH) + conv_b
    hf = h.astype(jnp.float32)
    mu = jnp.mean(hf, axis=-1, keepdims=True)
    var = jnp.mean(jnp.square(hf - mu), axis=-1, keepdims=True)
    hf = (hf - mu) * lax.rsqrt(var + 1e-5) * ln_g + ln_b
    return jax.nn.silu(hf).astype(u.dtype) @ conv_pw

def rotary(x, pos):
    half = HEAD_DIM // 2
    inv = ROPE_BASE ** (-jnp.arange(half, dtype=jnp.float32) / half)
    ang = pos[:, None] * inv[None, :]
    cos, sin = jnp.cos(ang), jnp.sin(ang)
    x1, x2 = x[..., :half], x[..., half:]
    return jnp.concatenate([x1 * cos - x2 * sin, x1 * sin + x2 * cos], axis=-1)

def retention(q, k, v, gate, gn_g):
    B, T, _ = q.shape
    heads = lambda a: a.astype(jnp.float32).reshape(B, T, RET_HEADS, HEAD_DIM).transpose(0, 2, 1, 3)
    q, k, v = heads(q), heads(k), heads(v)
    pos = jnp.arange(T, dtype=jnp.float32)
    q = rotary(q, pos)
    k = rotary(k, pos) * HEAD_DIM ** -0.5
    log_gamma = jnp.log1p(-jnp.exp2(-5.0 - jnp.arange(RET_HEADS, dtype=jnp.float32)))
    i = jnp.arange(RET_CHUNK, dtype=jnp.float32)
    rel = i[:, None] - i[None, :]
    decay = jnp.where(rel >= 0, jnp.exp(jnp.maximum(rel, 0.0)[None] * log_gamma[:, None, None]), 0.0)
    xi = jnp.exp((i + 1.0)[None, :] * log_gamma[:, None])
    zeta = jnp.exp((RET_CHUNK - 1.0 - i)[None, :] * log_gamma[:, None])
    g_chunk = jnp.exp(RET_CHUNK * log_gamma)
    nc = T // RET_CHUNK
    chunks = lambda a: a.reshape(B, RET_HEADS, nc, RET_CHUNK, HEAD_DIM).transpose(2, 0, 1, 3, 4)
    qc, kc, vc = chunks(q), chunks(k), chunks(v)
    intra = jnp.einsum('nbhqd,nbhkd->nbhqk', qc, kc) * decay[None, None]
    intra = jnp.einsum('nbhqk,nbhkd->nbhqd', intra, vc)

    def step(S, inp):
        qi, ki, vi = inp
        cross = jnp.einsum('bhqd,bhde->bhqe', qi, S) * xi[None, :, :, None]
        S = g_chunk[None, :, None, None] * S + jnp.einsum('bhkd,bhke->bhde', ki * zeta[None, :, :, None], vi)
        return S, cross

    S0 = jnp.zeros((B, RET_HEADS, HEAD_DIM, HEAD_DIM), jnp.float32)
    _, cross = lax.scan(step, S0, (qc, kc, vc))
    o = (intra + cross).transpose(1, 0, 3, 2, 4).reshape(B, T, RET_HEADS, HEAD_DIM)
    mu = jnp.mean(o, axis=-1, keepdims=True)
    var = jnp.mean(jnp.square(o - mu), axis=-1, keepdims=True)
    o = ((o - mu) * lax.rsqrt(var + 1e-5)).reshape(B, T, RET_W) * gn_g
    return (jax.nn.silu(gate.astype(jnp.float32)) * o).astype(gate.dtype)

def token_mixer(h, w_in, cmp_pe, cmp_w1, cmp_w2, conv_w, conv_b, conv_ln_g, conv_ln_b, conv_pw, ret_gn, w_out):
    proj = h @ w_in
    offs = np.cumsum(IN_SPLITS)[:-1].tolist()
    (q, k_c, v_c, k_s, v_s, k_w, v_w, gl, conv_in, rq, rk, rv, rg) = jnp.split(proj, offs, axis=-1)
    o_a = nsa_mixer(q, k_c, v_c, k_s, v_s, k_w, v_w, gl, cmp_pe, cmp_w1, cmp_w2)
    o_b = conformer_conv(conv_in, conv_w, conv_b, conv_ln_g, conv_ln_b, conv_pw)
    o_c = retention(rq, rk, rv, rg, ret_gn)
    return jnp.concatenate([o_a, o_b, o_c], axis=-1) @ w_out

def swiglu(h, w13, w2):
    a, b = jnp.split(h @ w13, 2, axis=-1)
    return (jax.nn.silu(a) * b) @ w2

def moe_ffn(h, router, w13, w2):
    B, T, D = h.shape
    N = B * T
    xf = h.reshape(N, D)
    logits = (xf @ router).astype(jnp.float32)
    top_logit, top_e = lax.top_k(logits, TOP_K)
    gates = jax.nn.softmax(top_logit, axis=-1)
    e_flat = top_e.reshape(-1)
    tok_flat = jnp.repeat(jnp.arange(N, dtype=jnp.int32), TOP_K)
    g_flat = gates.reshape(-1)
    order = jnp.argsort(e_flat)
    e_sorted = e_flat[order]
    counts = jnp.bincount(e_flat, length=N_EXPERTS)
    padded = ((counts + MOE_BLOCK - 1) // MOE_BLOCK) * MOE_BLOCK
    starts = jnp.cumsum(counts) - counts
    pends = jnp.cumsum(padded)
    pstarts = pends - padded
    dest = pstarts[e_sorted] + (jnp.arange(N * TOP_K) - starts[e_sorted])
    P = ((N * TOP_K + MOE_BLOCK - 1) // MOE_BLOCK) * MOE_BLOCK + N_EXPERTS * MOE_BLOCK
    buf_tok = jnp.full((P,), N, jnp.int32).at[dest].set(tok_flat[order])
    buf_gate = jnp.zeros((P,), jnp.float32).at[dest].set(g_flat[order])
    nblk = P // MOE_BLOCK
    blk_e = jnp.minimum(jnp.searchsorted(pends, jnp.arange(nblk) * MOE_BLOCK, side='right'), N_EXPERTS - 1)
    x_pad = jnp.concatenate([xf, jnp.zeros((1, D), xf.dtype)], axis=0)
    xb = x_pad[buf_tok].reshape(nblk, MOE_BLOCK, D)
    yb = lax.map(lambda a: swiglu(a[0], w13[a[1]], w2[a[1]]), (xb, blk_e))
    y = jax.ops.segment_sum(yb.reshape(P, D) * buf_gate[:, None].astype(yb.dtype), buf_tok, num_segments=N + 1)
    return y[:N].reshape(B, T, D)

def setup_inputs(seed: int = 0) -> dict:
    key = jax.random.key(seed)
    ks = jax.random.split(key, 20)
    L = DEPTH
    ND = (DEPTH + 1) // 2
    NM = DEPTH // 2
    nrm = lambda k, shape, s: jax.random.normal(k, shape, jnp.float32) * s
    return {
        'x': nrm(ks[0], (BATCH, SEQ, D_MODEL), 1.0),
        'ln_attn': 1.0 + nrm(ks[1], (L, D_MODEL), 0.1),
        'w_in': nrm(ks[2], (L, D_MODEL, D_IN), D_MODEL ** -0.5),
        'cmp_pe': nrm(ks[3], (L, 2, CMP_LEN, HEAD_DIM), 0.1),
        'cmp_w1': nrm(ks[4], (L, 2, CMP_LEN * HEAD_DIM, CMP_HIDDEN), (CMP_LEN * HEAD_DIM) ** -0.5),
        'cmp_w2': nrm(ks[5], (L, 2, CMP_HIDDEN, HEAD_DIM), CMP_HIDDEN ** -0.5),
        'conv_w': nrm(ks[6], (L, CONV_K, CONV_CH), CONV_K ** -0.5),
        'conv_b': nrm(ks[7], (L, CONV_CH), 0.02),
        'conv_ln_g': 1.0 + nrm(ks[8], (L, CONV_CH), 0.1),
        'conv_ln_b': nrm(ks[9], (L, CONV_CH), 0.02),
        'conv_pw': nrm(ks[10], (L, CONV_CH, CONV_CH), CONV_CH ** -0.5),
        'ret_gn': 1.0 + nrm(ks[11], (L, RET_W), 0.1),
        'w_out': nrm(ks[12], (L, D_MIX, D_MODEL), D_MIX ** -0.5),
        'ln_ffn': 1.0 + nrm(ks[13], (L, D_MODEL), 0.1),
        'ffn_w13': nrm(ks[14], (ND, D_MODEL, 2 * D_FF), D_MODEL ** -0.5),
        'ffn_w2': nrm(ks[15], (ND, D_FF, D_MODEL), D_FF ** -0.5),
        'router': nrm(ks[16], (NM, D_MODEL, N_EXPERTS), D_MODEL ** -0.5),
        'moe_w13': nrm(ks[17], (NM, N_EXPERTS, D_MODEL, 2 * D_FF), D_MODEL ** -0.5),
        'moe_w2': nrm(ks[18], (NM, N_EXPERTS, D_FF, D_MODEL), D_FF ** -0.5),
        'ln_final': 1.0 + nrm(ks[19], (D_MODEL,), 0.1),
    }

def reference(x, ln_attn, w_in, cmp_pe, cmp_w1, cmp_w2, conv_w, conv_b, conv_ln_g, conv_ln_b, conv_pw,
              ret_gn, w_out, ln_ffn, ffn_w13, ffn_w2, router, moe_w13, moe_w2, ln_final):
    for l in range(DEPTH):
        h = rmsnorm(x, ln_attn[l])
        x = x + token_mixer(h, w_in[l], cmp_pe[l], cmp_w1[l], cmp_w2[l], conv_w[l], conv_b[l],
                            conv_ln_g[l], conv_ln_b[l], conv_pw[l], ret_gn[l], w_out[l])
        h = rmsnorm(x, ln_ffn[l])
        if l % 2 == 0:
            x = x + swiglu(h, ffn_w13[l // 2], ffn_w2[l // 2])
        else:
            x = x + moe_ffn(h, router[l // 2], moe_w13[l // 2], moe_w2[l // 2])
    return rmsnorm(x, ln_final)


_drawn_inputs = setup_inputs


def setup_inputs(seed=0):
    import zlib

    import numpy as np

    out = dict(_drawn_inputs(seed))
    spreads = {}
    factors = {'conv_ln_b': 3.084}
    for name, (base, spread) in spreads.items():
        noise = np.random.default_rng([zlib.crc32(name.encode()), seed]).standard_normal(out[name].shape)
        drawn = base * np.exp(spread * noise) if base else spread * noise
        out[name] = __import__('jax').numpy.asarray(drawn.astype(out[name].dtype))
    for name, factor in factors.items():
        out[name] = (out[name] * factor).astype(out[name].dtype)
    return out
```

```python
from contextlib import ExitStack

import numpy as np

import concourse.bass as bass
from concourse import mybir

F32 = mybir.dt.float32
F32R = mybir.dt.float32r
I32 = mybir.dt.int32
ALU = mybir.AluOpType
ACT = mybir.ActivationFunctionType
AX = mybir.AxisListType

P = 128
D = 1024
T = 256
NT = T // P
KD = D // P
DEPTH = 2
HD = 64
HEADS = 8
HPG = 4
CMP_STRIDE, CMP_LEN, CMP_HID = 16, 32, 256
NBLK = T // CMP_STRIDE - CMP_LEN // CMP_STRIDE + 1
CB = 16
CONV_CH, CONV_K = 256, 31
NC = CONV_CH // P
RET_HEADS = 4
D_FF = 2816
FC = 256
STEPS = D_FF // FC
EXPERTS = 8
SCALE = HD ** -0.5
NEG = -1e30
EPS, LN_EPS = 1e-6, 1e-5
ARENA = 22330

SLOTS = 3
SLOT = 6144
FFN_ITEM = KD * 2 * FC + (FC // P) * D
MIX_ITEMS = (KD * 768, KD * 768, KD * 536, KD * 768, 16 * CMP_HID + 2 * P, 16 * CMP_HID + 2 * HD + 2 * CONV_CH,
             KD * 512, KD * 512)
MIX_OFF = [sum(MIX_ITEMS[:n]) * P for n in range(len(MIX_ITEMS) + 1)]
MIX_FILLS = [len([m for m in range(len(MIX_ITEMS)) if m % SLOTS == s]) for s in range(SLOTS)]
FFN_FILLS = [len([m for m in range(STEPS) if m % SLOTS == s]) for s in range(SLOTS)]

CONSTS = {}
CONST_COLS = 0
for _name, _n in (("ident", P), ("causal", P), ("cmp_add", NT * CB), ("cmp_keep", NT * CB), ("head_block", HEADS),
                  ("cos", NT * HD), ("sin", NT * HD), ("decay", RET_HEADS * T), ("before", P), ("ones", P),
                  ("slot", NT * P), ("earlier", EXPERTS * EXPERTS)):
    CONSTS[_name] = (CONST_COLS, _n)
    CONST_COLS += _n

PARAMS = {}
PARAM_COLS = 0
for _name, _n in (("ln_attn", KD), ("ln_ffn", KD), ("pe", 2 * 16), ("conv_w", NC * CONV_K), ("conv_b", NC),
                  ("conv_g", NC), ("conv_beta", NC), ("ret_gn", RET_HEADS * HD)):
    PARAMS[_name] = (PARAM_COLS, _n)
    PARAM_COLS += _n

UNITS = [(br, g, i, c, n) for br in range(2) for g in range(2) for i, c, n in ((0, 0, 4), (1, 0, 2), (1, 2, 2))]

CONV_PARTS = 8
MIXER = (
    [("norm", 0), ("q", 0), ("q", 1), ("ks", 0), ("score", 0), ("score", 1), ("kcv", 0), ("cg", 0), ("ca", 0),
     ("probT", 0), ("score", 2), ("probT", 1), ("score", 3), ("vsw", 0), ("gl", 0), ("pv", 0), ("pv", 1), ("rqk", 0), ("rqk", 1),
     ("conv", 0), ("probT", 2), ("score", 4), ("pv", 2), ("rvg", 0), ("rvg", 1), ("conv", 1),
     ("probT", 3), ("score", 5), ("pv", 3), ("hid", 0), ("hid", 1), ("conv", 2), ("probT", 4), ("score", 6),
     ("pv", 4), ("cmpkv", 0), ("retT", 0), ("retT", 1), ("probT", 5), ("score", 7), ("pv", 5), ("cscore", 0),
     ("conv", 3), ("probT", 6), ("score", 8), ("pv", 6), ("rets", 0), ("rets", 1), ("conv", 4), ("probT", 7),
     ("score", 9), ("pv", 7), ("rets", 2), ("rets", 3), ("cprobT", 0), ("conv", 5), ("probT", 8), ("score", 10),
     ("pv", 8), ("reto", 0), ("cpv", 0), ("cpv", 1), ("conv", 6), ("probT", 9), ("score", 11), ("pv", 9),
     ("conv", 7), ("probT", 10), ("pv", 10), ("convT", 0), ("probT", 11), ("pv", 11), ("retnorm", 0), ("convB", 0),
     ("attn_sum", 0), ("attn_sum", 1), ("conv_pw", 0), ("retcat", 0), ("out", 0), ("out", 1), ("norm", 1)])

PSUM_GROUPS = {"norm": 4, "q": 1, "ks": 1, "score": 1, "kcv": 1, "cg": 1, "ca": 1, "probT": 1, "vsw": 1, "pv": 1,
               "rqk": 1, "rvg": 1, "gl": 1, "hid": 1, "cmpkv": 1, "retT": 1, "cscore": 2, "rets": 1, "cprobT": 1,
               "reto": 1, "cpv": 1, "convT": 1, "convB": 1, "attn_sum": 1, "conv_pw": 1, "retcat": 1, "out": 2,
               "conv": 0, "retnorm": 0}
BANKS = 8
LAST_READ = (("ks", 0, 0), ("ca", 0, 0), ("rqk", 1, 0), ("rvg", 1, 0), ("cmpkv", 0, 0), ("conv_pw", 0, 0),
             ("out", 0, 1), ("out", 1, 1))
LAST_STEP = [max(j for j in range(STEPS) if j % SLOTS == s) for s in range(SLOTS)]
LAST_ITEM = [max(m for m in range(len(MIX_ITEMS)) if m % SLOTS == s) for s in range(SLOTS)]
GROUP = {}
_n = 0
for _l in range(DEPTH):
    for _stage, _k in MIXER:
        for _j in range(PSUM_GROUPS[_stage]):
            GROUP[(_l, _stage, _k, _j)] = (_n % BANKS, _n // BANKS + 1)
            _n += 1


def spread(ap, axis, n):
    u = ap.unsqueeze(axis)
    shape = list(u.shape)
    shape[axis] = n
    return u.broadcast_to(shape)


def hybrid_trunk_kernel(nc, x_in, consts_in, params_in, mix_in, ffn_in, moe_in, router_in, final_in, out):
    with ExitStack() as ctx:
        def sb(name, shape, dt=F32):
            return ctx.enter_context(nc.sbuf_tensor(name, shape, dt))

        def sem(name):
            return ctx.enter_context(nc.semaphore(name))

        ps = ctx.enter_context(nc.psum_tensor("ps", [P, BANKS, 512], F32))
        ring = sb("ring", [P, SLOTS, SLOT])
        cst = sb("cst", [P, CONST_COLS])
        par = sb("par", [P, DEPTH, PARAM_COLS])
        router = sb("router", [P, KD, EXPERTS])
        gfin = sb("gfin", [P, D])
        x = sb("x", [P, NT, D])
        xn = sb("xn", [P, NT, D])
        hT = sb("hT", [P, KD, T])
        stat = sb("stat", [P, 4, NT])

        arena = sb("arena", [P, ARENA])

        def arena_of():
            at = [0]

            def view(name, shape):
                n = int(np.prod(shape[1:]))
                v = arena[:, at[0]:at[0] + n]
                at[0] += n
                assert at[0] <= ARENA, (name, at[0])
                dims = " ".join(f"a{i}" for i in range(1, len(shape)))
                return v.rearrange(f"p ({dims}) -> p {dims}", **{f"a{i}": shape[i] for i in range(1, len(shape))})
            return view

        mix = arena_of()
        qT = mix("qT", [P, HPG, T])
        kT = mix("kT", [P, 2, T])
        vv = mix("vv", [P, NT, 2, 2, HD])
        gates = mix("gates", [P, NT, HEADS, 3])
        prob = mix("prob", [P, 3, 512])
        probT = mix("probT", [P, 3, 512])
        amax = mix("amax", [P, len(UNITS), HPG])
        nmax = mix("nmax", [P, len(UNITS), HPG])
        asum = mix("asum", [P, len(UNITS), HPG])
        arec = mix("arec", [P, len(UNITS), HPG])
        awgt = mix("awgt", [P, len(UNITS), HPG])
        obr = mix("obr", [P, 3, NT, HEADS, HD])
        catT = mix("catT", [P, KD, T])
        blocks = sb("blocks", [P, 2, 2, 8, 2, CB])
        hid = mix("hid", [P, 2, 2, 2 * CB])
        hidv = mix("hidv", [P, 4, HPG, CB])
        kc = mix("kc", [P, 2 * CB])
        vblk = mix("vblk", [P, HEADS, HD])
        cs = mix("cs", [P, NT, HEADS, CB])
        cs2 = mix("cs2", [P, NT, HEADS, CB])
        cprob = mix("cprob", [P, NT, HEADS, CB])
        cstat = mix("cstat", [P, 4, NT, HEADS])
        cprobT = mix("cprobT", [P, NT, P])
        sig = mix("sig", [P, NC, T])
        hc = sb("hc", [P, NC, CONV_K - 1 + T])
        cacc = mix("cacc", [P, 2, NC, T])
        cln = mix("cln", [P, NT, CONV_CH])
        csq = mix("csq", [P, NT, CONV_CH])
        clst = mix("clst", [P, 5, NT])
        cact = mix("cact", [P, NC, T])
        rqk = mix("rqk", [P, NT, 2 * RET_HEADS, HD])
        rot = mix("rot", [P, 2, 2 * RET_HEADS, HD])
        rT = mix("rT", [P, 4, T])
        rv = mix("rv", [P, NT, RET_HEADS, HD])
        rgate = mix("rgate", [P, NT, RET_HEADS, HD])
        rp0 = mix("rp0", [P, RET_HEADS, T])
        rp1 = mix("rp1", [P, RET_HEADS, P])
        ro = mix("ro", [P, NT, RET_HEADS, HD])
        rsq = mix("rsq", [P, NT, RET_HEADS, HD])
        rst = mix("rst", [P, 5, NT, RET_HEADS])

        ffn = arena_of()
        silu = ffn("silu", [P, 3, FC])
        gated = ffn("gated", [P, 3, FC])
        gT = ffn("gT", [P, 3, FC // P, P])
        logit = ffn("logit", [P, NT, EXPERTS])
        rcmp = ffn("rcmp", [P, 3, NT, EXPERTS, EXPERTS])
        rwork = ffn("rwork", [P, 4, NT, EXPERTS])
        rmax = ffn("rmax", [P, 2, NT])
        sel = ffn("sel", [P, NT, EXPERTS + 1])
        gate = ffn("gate", [P, NT, EXPERTS + 1])
        rank = ffn("rank", [P, NT, EXPERTS + 1])
        cnt = ffn("cnt", [P, EXPERTS])
        cmx = ffn("cmx", [P, 1])
        over = sb("over", [P, 1], I32)
        pick = ffn("pick", [P, NT, P])
        spill = ffn("spill", [P, NT, P])
        spillT = ffn("spillT", [P, T])
        xeT = ffn("xeT", [P, KD, P])
        ye = ffn("ye", [P, 2, 512])
        res = xn

        bank_full = [sem(f"bank_full{b}") for b in range(BANKS)]
        bank_free = [sem(f"bank_free{b}") for b in range(BANKS)]
        slot_full = [sem(f"slot_full{s}") for s in range(SLOTS)]
        s_in = sem("s_in")
        s_x = sem("s_x")
        s_zero = sem("s_zero")
        s_ss = sem("s_ss")
        s_ms = sem("s_ms")
        s_root = sem("s_root")
        s_xn = sem("s_xn")
        s_amax = sem("s_amax")
        s_exp = sem("s_exp")
        s_cs2 = sem("s_cs2")
        s_cexp = sem("s_cexp")
        s_cprob = sem("s_cprob")
        s_conv = sem("s_conv")
        s_cvar = sem("s_cvar")
        s_croot = sem("s_croot")
        s_cln = sem("s_cln")
        s_rvar = sem("s_rvar")
        s_rroot = sem("s_rroot")
        s_ret = sem("s_ret")
        s_osum = sem("s_osum")
        v_done = sem("v_done")
        a_done = sem("a_done")
        s_up = sem("s_up")
        s_silu = sem("s_silu")
        s_gated = sem("s_gated")
        s_gtp = sem("s_gtp")
        s_gT = sem("s_gT")
        s_down = sem("s_down")
        s_dense = sem("s_dense")
        s_logit = sem("s_logit")
        s_lcopy = sem("s_lcopy")
        s_m1 = sem("s_m1")
        s_rexp = sem("s_rexp")
        s_sel = sem("s_sel")
        s_rankp = sem("s_rankp")
        s_over = sem("s_over")
        s_pick = sem("s_pick")
        s_spill = sem("s_spill")
        s_gather = sem("s_gather")
        s_xeT = sem("s_xeT")
        s_spt = sem("s_spt")
        s_sptc = sem("s_sptc")
        s_ye = sem("s_ye")
        s_scat = sem("s_scat")
        s_xadd = sem("s_xadd")
        s_last = sem("s_last")
        s_res = sem("s_res")
        s_out = sem("s_out")

        def const(name, n=None):
            a, w = CONSTS[name]
            return cst[:, a:a + (n or w)]

        def param(l, name):
            a, w = PARAMS[name]
            return par[:, l, a:a + w]

        ident = const("ident")
        INPUTS = 4

        def bank(l, stage, k=0, j=0):
            return ps[:, GROUP[(l, stage, k, j)][0], :]

        def full(eng, l, stage, k=0, j=0):
            b, n = GROUP[(l, stage, k, j)]
            eng.wait_ge(bank_full[b], n)

        def freed(eng, l, stage, k=0, j=0):
            b, n = GROUP[(l, stage, k, j)]
            eng.wait_ge(bank_free[b], n)

        def is_full(ins, l, stage, k=0, j=0):
            ins.then_inc(bank_full[GROUP[(l, stage, k, j)][0]], 1)

        def is_free(ins, l, stage, k=0, j=0):
            ins.then_inc(bank_free[GROUP[(l, stage, k, j)][0]], 1)

        def mix_fill(l, m):
            s = m % SLOTS
            return l * (MIX_FILLS[s] + FFN_FILLS[s]) + m // SLOTS + 1

        def ffn_base(l, s):
            return l * (MIX_FILLS[s] + FFN_FILLS[s]) + MIX_FILLS[s]

        def item(m):
            return ring[:, m % SLOTS, 0:MIX_ITEMS[m]]

        block = ctx.enter_context(nc.Block())

        @block.sync
        def _(sp):
            sp.dma_start(x[:], x_in.rearrange("(i p) d -> p i d", p=P)).then_inc(s_x, 16)
            sp.dma_start(cst[:], consts_in).then_inc(s_in, 16)
            sp.dma_start(par[:], params_in).then_inc(s_in, 16)

            def ffn_items(l, u0, tiles, src):
                for j in range(STEPS):
                    s = j % SLOTS
                    if j >= SLOTS:
                        sp.wait_ge(s_down, u0 + tiles * (j - SLOTS + 1))
                    else:
                        full(sp, l, *LAST_READ[LAST_ITEM[s]])
                        if l:
                            sp.wait_ge(s_down, u0 - STEPS + LAST_STEP[s] + 1)
                    sp.dma_start(ring[:, s, :], src(j)).then_inc(slot_full[s], 16)

            for l in range(DEPTH):
                for m, n in enumerate(MIX_ITEMS):
                    s = m % SLOTS
                    if m >= SLOTS:
                        full(sp, l, *LAST_READ[m - SLOTS])
                    elif l:
                        sp.wait_ge(s_down, NT * (LAST_STEP[s] + 1))
                    src = mix_in[l, MIX_OFF[m]:MIX_OFF[m + 1]].rearrange("(p n) -> p n", p=P)
                    sp.dma_start(item(m), src).then_inc(slot_full[s], 16)
                    if l == 0 and m == 1:
                        sp.dma_start(router[:], router_in).then_inc(s_in, 16)
                        sp.dma_start(gfin[:], final_in).then_inc(s_in, 16)
                if l == 0:
                    ffn_items(0, 0, NT, lambda j: ffn_in[j])
                else:
                    with sp.Fori(0, EXPERTS) as e:
                        ffn_items(1, NT * STEPS + e * STEPS, 1, lambda j: moe_in[e * STEPS + j])
            sp.wait_ge(s_over, 1)
            more = sp.value_load(over[0:1, 0:1], min_val=0, max_val=1)
            with sp.If(more > 0):
                with sp.Fori(0, EXPERTS) as e:
                    ffn_items(1, NT * STEPS + (EXPERTS + e) * STEPS, 1, lambda j: moe_in[e * STEPS + j])
            for i in range(NT):
                sp.wait_ge(s_res, i + 1)
                sp.dma_start(out[i * P:(i + 1) * P, :], res[:, i, :]).then_inc(s_out, 16)
            sp.wait_ge(s_out, NT * 16)

        @block.tensor
        def _(pe):
            def mm(o, lhsT, rhs, first, last):
                return nc.tensor.matmul(o, lhsT, rhs, start=first, stop=last, skip_group_check=True)

            def flip(o, a):
                return nc.tensor.transpose(o, a, ident)

            def begin(l, stage, k=0, j=0):
                b, n = GROUP[(l, stage, k, j)]
                if n > 1:
                    pe.wait_ge(bank_free[b], n - 1)
                return ps[:, b, :]

            def landed(l, m):
                pe.wait_ge(slot_full[m % SLOTS], 16 * mix_fill(l, m))

            def width_major(o, m, width, col):
                w = item(m).rearrange("p (k n) -> p k n", k=KD)
                for k in range(KD):
                    last = mm(o, w[:, k, col:col + P], hT[:, k, :], k == 0, k == KD - 1)
                return last

            def token_major(o, m, i, col, n):
                w = item(m).rearrange("p (k n) -> p k n", k=KD)
                for k in range(KD):
                    last = mm(o, hT[:, k, i * P:(i + 1) * P], w[:, k, col:col + n], k == 0, k == KD - 1)
                return last

            def mixer(l):
                for stage, k in MIXER:
                    if stage == "norm":
                        for i in range(NT):
                            pe.wait_ge(s_xn, (2 * l + k) * NT + i + 1)
                            for half in range(2):
                                o = begin(l, "norm", k, 2 * i + half)
                                for q in range(4):
                                    c = 4 * half + q
                                    last = flip(o[:, q * P:(q + 1) * P], xn[:, i, c * P:(c + 1) * P])
                                is_full(last, l, "norm", k, 2 * i + half)
                    elif stage == "q":
                        o = begin(l, stage, k)
                        if k == 0:
                            for j in range(4):
                                freed(pe, l, "norm", 0, j)
                            landed(l, 0)
                        width_major(o[:, 0:T], 0, 768, 2 * k * P)
                        is_full(width_major(o[:, T:2 * T], 0, 768, (2 * k + 1) * P), l, stage, k)
                    elif stage == "ks":
                        o = begin(l, stage)
                        width_major(o[:, 0:T], 0, 768, 4 * P)
                        is_full(width_major(o[:, T:2 * T], 0, 768, 5 * P), l, stage)
                    elif stage in ("kcv", "ca", "cg"):
                        o = begin(l, stage)
                        if stage == "kcv":
                            landed(l, 1)
                        col = {"kcv": 0, "ca": 2 * P, "cg": 4 * P}[stage]
                        width_major(o[:, 0:T], 1, 768, col)
                        is_full(width_major(o[:, T:2 * T], 1, 768, col + P), l, stage)
                    elif stage == "vsw":
                        o = begin(l, stage)
                        landed(l, 2)
                        for i in range(NT):
                            last = token_major(o[:, i * 256:(i + 1) * 256], 2, i, 0, 256)
                        is_full(last, l, stage)
                    elif stage == "rqk":
                        o = begin(l, stage, k)
                        if k == 0:
                            landed(l, 3)
                        token_major(o[:, 0:256], 3, k, 0, 256)
                        is_full(token_major(o[:, 256:512], 2, k, 280, 256), l, stage, k)
                    elif stage == "rvg":
                        is_full(token_major(begin(l, stage, k), 3, k, 256, 512), l, stage, k)
                    elif stage == "gl":
                        o = begin(l, stage)
                        for i in range(NT):
                            last = token_major(o[:, i * 24:(i + 1) * 24], 2, i, 256, 24)
                        is_full(last, l, stage)
                    elif stage == "score":
                        br, g, i, c0, n = UNITS[k]
                        keys = (i + 1) * P
                        o = begin(l, stage, k)
                        if k == 0:
                            freed(pe, l, "ks")
                            freed(pe, l, "q", 0)
                            freed(pe, l, "q", 1)
                        ov = o[:, 0:n * keys].rearrange("p (n k) -> p n k", n=n)
                        mm(ov[:, :, i * P:keys], ident, spread(const("causal"), 1, n), True, False)
                        lo = g * HD
                        for c in range(n):
                            last = mm(o[:, c * keys:(c + 1) * keys], qT[lo:lo + HD, c0 + c, i * P:(i + 1) * P],
                                      kT[lo:lo + HD, br, 0:keys], False, c == n - 1)
                        is_full(last, l, stage, k)
                    elif stage == "probT":
                        br, g, i, c0, n = UNITS[k]
                        o = begin(l, stage, k)
                        pe.wait_ge(s_exp, l * len(UNITS) + k + 1)
                        for q in range(4):
                            last = flip(o[:, q * P:(q + 1) * P], prob[:, k % 3, q * P:(q + 1) * P])
                        is_full(last, l, stage, k)
                    elif stage == "pv":
                        br, g, i, c0, n = UNITS[k]
                        o = begin(l, stage, k)
                        freed(pe, l, "probT", k)
                        if k == 0:
                            freed(pe, l, "vsw")
                        for c in range(n):
                            for t in range(i + 1):
                                q = c * (i + 1) + t
                                last = mm(o[:, c * HD:(c + 1) * HD], probT[:, k % 3, q * P:(q + 1) * P],
                                          vv[:, t, br, g, :], t == 0, t == i)
                        is_full(last, l, stage, k)
                    elif stage == "hid":
                        o = begin(l, stage, k)
                        landed(l, 4 + k)
                        if k == 0:
                            freed(pe, l, "kcv")
                        w = item(4 + k)[:, 0:16 * CMP_HID].rearrange("p (j n) -> p j n", j=16)
                        for m in range(2):
                            for j in range(16):
                                last = mm(o[:, m * 32:(m + 1) * 32], w[:, j, m * P:(m + 1) * P],
                                          blocks[:, k, j // 8, j % 8, :, :], j == 0, j == 15)
                        is_full(last, l, stage, k)
                    elif stage == "cmpkv":
                        o = begin(l, stage)
                        freed(pe, l, "hid", 0)
                        freed(pe, l, "hid", 1)
                        wk = item(4)[:, 16 * CMP_HID:].rearrange("p (m n) -> p m n", m=2)
                        wv = item(5)[:, 16 * CMP_HID:16 * CMP_HID + 2 * HD].rearrange("p (m n) -> p m n", m=2)
                        for m in range(2):
                            mm(o[:, 0:2 * CB], wk[:, m, :], hid[:, 0, m, :], m == 0, m == 1)
                        for m in range(2):
                            last = mm(o[:, HD:2 * HD], hidv[:, 2 * m:2 * m + 2, :, :], wv[:, m, :], m == 0, m == 1)
                        is_full(last, l, stage)
                    elif stage == "cscore":
                        for g in range(2):
                            o = begin(l, stage, 0, g)
                            if g == 0:
                                freed(pe, l, "cmpkv")
                            lo = g * HD
                            for i in range(NT):
                                for c in range(HPG):
                                    q = i * HPG + c
                                    last = mm(o[:, q * CB:(q + 1) * CB], qT[lo:lo + HD, c, i * P:(i + 1) * P],
                                              kc[lo:lo + HD, g * CB:(g + 1) * CB], True, True)
                            is_full(last, l, stage, 0, g)
                    elif stage == "cprobT":
                        o = begin(l, stage)
                        pe.wait_ge(s_cprob, l + 1)
                        for i in range(NT):
                            last = flip(o[:, i * P:(i + 1) * P], cprob[:, i, :, :].rearrange("p h c -> p (h c)"))
                        is_full(last, l, stage)
                    elif stage == "cpv":
                        o = begin(l, stage, k)
                        if k == 0:
                            freed(pe, l, "cprobT")
                        last = mm(o, cprobT[:, k, :], vblk[:].rearrange("p h d -> p (h d)"), True, True)
                        is_full(last, l, stage, k)
                    elif stage == "retT":
                        o = begin(l, stage, k)
                        freed(pe, l, "rqk", k)
                        for q in range(4):
                            last = flip(o[:, q * P:(q + 1) * P],
                                        rqk[:, k, 2 * q:2 * q + 2, :].rearrange("p h d -> p (h d)"))
                        is_full(last, l, stage, k)
                    elif stage == "rets":
                        b, t = k % 2, k // 2
                        o = begin(l, stage, k)
                        if k == 0:
                            freed(pe, l, "retT", 0)
                            freed(pe, l, "retT", 1)
                        lo, n = b * HD, T - t * P
                        for u in range(2):
                            last = mm(o[:, u * n:(u + 1) * n], rT[lo:lo + HD, 2 + u, t * P:(t + 1) * P],
                                      rT[lo:lo + HD, u, t * P:T], True, True)
                        is_full(last, l, stage, k)
                    elif stage == "reto":
                        o = begin(l, stage)
                        for j in range(4):
                            freed(pe, l, "rets", j)
                        freed(pe, l, "rvg", 0)
                        freed(pe, l, "rvg", 1)
                        for h in range(RET_HEADS):
                            mm(o[:, h * HD:(h + 1) * HD], rp0[:, h, 0:P], rv[:, 0, h, :], True, True)
                        for h in range(RET_HEADS):
                            oh = o[:, 256 + h * HD:256 + (h + 1) * HD]
                            mm(oh, rp0[:, h, P:T], rv[:, 0, h, :], True, False)
                            last = mm(oh, rp1[:, h, :], rv[:, 1, h, :], False, True)
                        is_full(last, l, stage)
                    elif stage == "convT":
                        o = begin(l, stage)
                        pe.wait_ge(s_conv, l + 1)
                        for i in range(NT):
                            for c in range(NC):
                                q = i * NC + c
                                last = flip(o[:, q * P:(q + 1) * P], cacc[:, 0, c, i * P:(i + 1) * P])
                        is_full(last, l, stage)
                    elif stage == "convB":
                        o = begin(l, stage)
                        pe.wait_ge(s_cln, l + 1)
                        for c in range(NC):
                            for i in range(NT):
                                q = c * NT + i
                                last = flip(o[:, q * P:(q + 1) * P], cln[:, i, c * P:(c + 1) * P])
                        is_full(last, l, stage)
                    elif stage == "conv_pw":
                        o = begin(l, stage)
                        freed(pe, l, "convB")
                        w = item(5)[:, 16 * CMP_HID + 2 * HD:].rearrange("p (c n) -> p c n", c=NC)
                        for m in range(NC):
                            for c in range(NC):
                                last = mm(o[:, m * T:(m + 1) * T], w[:, c, m * P:(m + 1) * P], cact[:, c, :],
                                          c == 0, c == NC - 1)
                        is_full(last, l, stage)
                    elif stage == "attn_sum":
                        o = begin(l, stage, k)
                        pe.wait_ge(s_osum, l * NT + k + 1)
                        for q in range(4):
                            last = flip(o[:, q * P:(q + 1) * P],
                                        obr[:, 0, k, 2 * q:2 * q + 2, :].rearrange("p h d -> p (h d)"))
                        is_full(last, l, stage, k)
                    elif stage == "retcat":
                        o = begin(l, stage)
                        pe.wait_ge(s_ret, l + 1)
                        for m in range(2):
                            for i in range(NT):
                                q = m * NT + i
                                last = flip(o[:, q * P:(q + 1) * P],
                                            ro[:, i, 2 * m:2 * m + 2, :].rearrange("p h d -> p (h d)"))
                        is_full(last, l, stage)
                    elif stage == "out":
                        w = item(6 + k).rearrange("p (k n) -> p k n", k=KD)
                        for i in range(NT):
                            o = begin(l, stage, k, i)
                            if k == 0 and i == 0:
                                for kk in range(NT):
                                    freed(pe, l, "attn_sum", kk)
                                freed(pe, l, "conv_pw")
                                freed(pe, l, "retcat")
                            if i == 0:
                                landed(l, 6 + k)
                            for c in range(KD):
                                last = mm(o, catT[:, c, i * P:(i + 1) * P], w[:, c, :], c == 0, c == KD - 1)
                            is_full(last, l, stage, k, i)

            def up(b, i, s, lhsT, half):
                w = ring[:, s, 0:KD * 2 * FC].rearrange("p (k n) -> p k n", k=KD)
                for k in range(4 * half, 4 * half + 4):
                    last = mm(ps[:, b, :], lhsT[:, k, i * P:(i + 1) * P], w[:, k, :], k == 0, k == KD - 1)
                if half:
                    last.then_inc(s_up, 1)

            def turn(b, u):
                pe.wait_ge(s_gated, u + 1)
                if not isinstance(u, int) or u > 0:
                    pe.wait_ge(s_gT, u)
                for c in range(FC // P):
                    last = flip(ps[:, 3, c * P:(c + 1) * P], gated[:, b, c * P:(c + 1) * P])
                last.then_inc(s_gtp, 1)

            def down(b, u, s, y0, first, final):
                pe.wait_ge(s_gT, u + 1)
                w = ring[:, s, KD * 2 * FC:].rearrange("p (c n) -> p c n", c=FC // P)
                for c in range(FC // P):
                    for n in range(2):
                        last = mm(ps[:, y0 + n, :], gT[:, b, c, :], w[:, c, n * 512:(n + 1) * 512],
                                  first and c == 0, final and c == FC // P - 1)
                last.then_inc(s_down, 1)

            def steps(tiles, lhsT, u0, base, before_sums=None):
                def unit(j, g, i):
                    v = j * tiles + i
                    u = u0 + v + g * (SLOTS * tiles)
                    if i == 0:
                        pe.wait_ge(slot_full[j % SLOTS], 16 * (base[j % SLOTS] + (j // SLOTS + 1) + g))
                    if not isinstance(u, int) or u > 1:
                        pe.wait_ge(s_gated, u - 1)
                    up(v % 3, i, j % SLOTS, lhsT, 0)
                    if v:
                        turn((v - 1) % 3, u - 1)
                    up(v % 3, i, j % SLOTS, lhsT, 1)
                    if v == 1 and before_sums is not None:
                        before_sums()
                    if v:
                        jp, ip = divmod(v - 1, tiles)
                        down((v - 1) % 3, u - 1, jp % SLOTS, 4 + 2 * ip, jp == 0, False)

                for j in range(2):
                    for i in range(tiles):
                        unit(j, 0, i)
                with pe.Fori(0, (STEPS - 2) // SLOTS) as g:
                    for j in range(2, 2 + SLOTS):
                        for i in range(tiles):
                            unit(j, g, i)

            def last_down(tiles, u0):
                v = tiles * STEPS - 1
                turn(v % 3, u0 + v)
                down(v % 3, u0 + v, (STEPS - 1) % SLOTS, 4 + 2 * (tiles - 1), False, True)

            def dense():
                for q in range(4):
                    freed(pe, 0, "norm", 1, q)
                steps(NT, hT, 0, [ffn_base(0, s) for s in range(SLOTS)])
                last_down(NT, 0)

            def gather(n):
                pe.wait_ge(s_pick, n + 1)
                for half in range(2):
                    for q in range(4):
                        c = 4 * half + q
                        for i in range(NT):
                            last = mm(ps[:, 6 + half, q * P:(q + 1) * P], xn[:, i, c * P:(c + 1) * P],
                                      pick[:, i, :], i == 0, i == NT - 1)
                    last.then_inc(s_gather, 1)

            def experts(rnd):
                n0 = rnd * (EXPERTS + 1)
                if rnd:
                    pe.wait_ge(s_xadd, 4 * EXPERTS + 1)
                gather(n0)
                with pe.Fori(0, EXPERTS) as e:
                    ex = e + rnd * EXPERTS
                    ue = NT * STEPS + ex * STEPS
                    pe.wait_ge(s_xeT, 2 * (n0 + e) + 2)
                    steps(1, xeT, ue, [ffn_base(1, s) + FFN_FILLS[s] * ex for s in range(SLOTS)],
                          lambda: pe.wait_ge(s_ye, 2 * ex + 1))
                    pe.wait_ge(s_xadd, 4 * ex + 1)
                    gather(n0 + e + 1)
                    last_down(1, ue)
                    pe.wait_ge(s_spill, ex + 1)
                    pe.wait_ge(s_gT, ue + STEPS)
                    for i in range(NT):
                        last = flip(ps[:, 3, i * P:(i + 1) * P], spill[:, i, :])
                    last.then_inc(s_spt, 1)
                    pe.wait_ge(s_sptc, ex + 1)
                    pe.wait_ge(s_xeT, 2 * (n0 + e) + 4)
                    for i in range(NT):
                        for n in range(2):
                            if i == 0:
                                pe.wait_ge(s_ye, 2 * ex + (n + 2))
                            else:
                                pe.wait_ge(s_xadd, 4 * ex + (n + 2))
                            mm(ps[:, 6 + n, :], spillT[:, i * P:(i + 1) * P], ye[:, n, :], True, True)\
                                .then_inc(s_scat, 1)

            for s in (s_scat, s_spt):
                pe.nop().then_inc(s, 1)
            pe.wait_ge(s_in, INPUTS * 16)
            mixer(0)
            dense()
            mixer(1)
            for q in range(4):
                freed(pe, 1, "norm", 1, q)
            for i in range(NT):
                for k in range(KD):
                    last = mm(ps[:, 0, i * EXPERTS:(i + 1) * EXPERTS], hT[:, k, i * P:(i + 1) * P], router[:, k, :],
                              k == 0, k == KD - 1)
            last.then_inc(s_logit, 1)
            pe.wait_ge(s_sel, 1)
            n = EXPERTS + 1
            mm(ps[:, 1, 0:n], const("before"), sel[:, 0, :], True, True)
            mm(ps[:, 1, n:2 * n], const("before"), sel[:, 1, :], True, False)
            mm(ps[:, 1, n:2 * n], const("ones"), sel[:, 0, :], False, True)
            mm(ps[:, 1, 2 * n:3 * n], const("ones"), sel[:, 0, :], True, False)
            mm(ps[:, 1, 2 * n:3 * n], const("ones"), sel[:, 1, :], False, True).then_inc(s_rankp, 1)
            pe.wait_ge(s_over, 1)
            experts(0)
            more = pe.value_load(over[0:1, 0:1], min_val=0, max_val=1)
            with pe.If(more > 0):
                experts(1)

        @block.scalar
        def _(act):
            A = nc.scalar.activation

            def rms_squares(n):
                for i in range(NT):
                    A(xn[:, i, :], x[:, i, :], ACT.Square, accum_out=stat[:, 0, i:i + 1]).then_inc(s_ss, 1)
                act.wait_ge(s_ms, n + 1)
                A(stat[:, 2, :], stat[:, 1, :], ACT.Sqrt).then_inc(s_root, 1)

            def mixer(l):
                for stage, k in MIXER:
                    if stage == "norm":
                        if k == 0 and l == 0:
                            act.wait_ge(s_x, 16)
                        elif k == 0:
                            act.wait_ge(s_dense, 4)
                        else:
                            for q in range(4):
                                freed(act, l, "out", q // 2, q % 2)
                        rms_squares(2 * l + k)
                    elif stage == "q":
                        full(act, l, stage, k)
                        is_free(A(qT[:, 2 * k:2 * k + 2, :], bank(l, stage, k).rearrange("p (c t) -> p c t", c=2),
                                  ACT.Copy), l, stage, k)
                    elif stage == "cg":
                        full(act, l, stage)
                        is_free(A(sig[:], bank(l, stage).rearrange("p (c t) -> p c t", c=NC), ACT.Sigmoid), l, stage)
                    elif stage == "vsw":
                        full(act, l, stage)
                        is_free(A(vv[:].rearrange("p i b g d -> p (i b g d)"), bank(l, stage), ACT.Copy), l, stage)
                    elif stage == "rvg":
                        full(act, l, stage, k)
                        o = bank(l, stage, k)
                        A(rv[:, k, :, :].rearrange("p h d -> p (h d)"), o[:, 0:256], ACT.Copy)
                        is_free(A(rgate[:, k, :, :].rearrange("p h d -> p (h d)"), o[:, 256:512], ACT.Silu),
                                l, stage, k)
                    elif stage == "gl":
                        full(act, l, stage)
                        is_free(A(gates[:].rearrange("p i h b -> p (i h b)"), bank(l, stage)[:, 0:NT * 24],
                                  ACT.Sigmoid), l, stage)
                    elif stage == "score":
                        br, g, i, c0, n = UNITS[k]
                        keys = (i + 1) * P
                        act.wait_ge(s_amax, l * len(UNITS) + k + 1)
                        if k >= 3:
                            full(act, l, "probT", k - 3)
                        for c in range(n):
                            last = A(prob[:, k % 3, c * keys:(c + 1) * keys],
                                     bank(l, stage, k)[:, c * keys:(c + 1) * keys], ACT.Exp,
                                     bias=nmax[:, k, c:c + 1], scale=SCALE, accum_out=asum[:, k, c:c + 1])
                        last.then_inc(s_exp, 1)
                        act.wait_ge(s_exp, l * len(UNITS) + k + 1)
                        is_free(act.nop(), l, stage, k)
                    elif stage == "probT":
                        if k >= 3:
                            full(act, l, "pv", k - 3)
                        full(act, l, stage, k)
                        is_free(A(probT[:, k % 3, :], bank(l, stage, k), ACT.Copy), l, stage, k)
                    elif stage == "hid":
                        full(act, l, stage, k)
                        o = bank(l, stage, k)[:, 0:64]
                        if k == 0:
                            ins = A(hid[:, 0, :, :].rearrange("p m n -> p (m n)"), o, ACT.Silu)
                        else:
                            ins = A(hidv[:], spread(o.rearrange("p (q c) -> p q c", q=4), 2, HPG), ACT.Silu)
                        is_free(ins, l, stage, k)
                    elif stage == "cscore":
                        act.wait_ge(s_cs2, l + 1)
                        A(cs[:], cs2[:], ACT.Exp).then_inc(s_cexp, 1)
                    elif stage == "cprobT":
                        full(act, l, stage)
                        is_free(A(cprobT[:], bank(l, stage)[:, 0:T].rearrange("p (i q) -> p i q", i=NT), ACT.Copy),
                                l, stage)
                    elif stage == "cpv":
                        full(act, l, stage, k)
                        is_free(A(obr[:, 2, k, :, :].rearrange("p h d -> p (h d)"), bank(l, stage, k), ACT.Copy),
                                l, stage, k)
                    elif stage == "retT":
                        full(act, l, stage, k)
                        is_free(A(rT[:, :, k * P:(k + 1) * P], bank(l, stage, k).rearrange("p (q t) -> p q t", q=4),
                                  ACT.Copy), l, stage, k)
                    elif stage == "convT":
                        act.wait_ge(s_cvar, l + 1)
                        A(clst[:, 3, :], clst[:, 2, :], ACT.Sqrt).then_inc(s_croot, 1)
                    elif stage == "retnorm":
                        act.wait_ge(s_rvar, l + 1)
                        A(rst[:, 3, :, :], rst[:, 2, :, :], ACT.Sqrt).then_inc(s_rroot, 1)
                    elif stage == "convB":
                        full(act, l, stage)
                        g, b = param(l, "conv_g"), param(l, "conv_beta")
                        for c in range(NC):
                            last = A(cact[:, c, :], bank(l, stage)[:, c * T:(c + 1) * T], ACT.Silu,
                                     bias=b[:, c:c + 1], scale=g[:, c:c + 1])
                        is_free(last, l, stage)
                    elif stage == "attn_sum":
                        full(act, l, stage, k)
                        is_free(A(catT[:, 0:4, k * P:(k + 1) * P],
                                  bank(l, stage, k).rearrange("p (q t) -> p q t", q=4), ACT.Copy), l, stage, k)
                    elif stage in ("conv_pw", "retcat"):
                        full(act, l, stage)
                        m = 4 if stage == "conv_pw" else 6
                        is_free(A(catT[:, m:m + 2, :], bank(l, stage).rearrange("p (q t) -> p q t", q=2), ACT.Copy),
                                l, stage)

            def turned(b, u):
                if not isinstance(u, int) or u > 1:
                    act.wait_ge(s_down, u - 1)
                act.wait_ge(s_gtp, u + 1)
                A(gT[:, b, :, :], ps[:, 3, 0:FC].rearrange("p (c t) -> p c t", c=FC // P), ACT.Copy)\
                    .then_inc(s_gT, 1)

            def steps(tiles, u0):
                def unit(j, g, i):
                    v = j * tiles + i
                    u = u0 + v + g * (SLOTS * tiles)
                    if v:
                        turned((v - 1) % 3, u - 1)
                    if not isinstance(u, int) or u > 1:
                        act.wait_ge(s_gated, u - 1)
                    act.wait_ge(s_up, u + 1)
                    A(silu[:, v % 3, :], ps[:, v % 3, 0:FC], ACT.Silu).then_inc(s_silu, 1)

                for j in range(2):
                    for i in range(tiles):
                        unit(j, 0, i)
                with act.Fori(0, (STEPS - 2) // SLOTS) as g:
                    for j in range(2, 2 + SLOTS):
                        for i in range(tiles):
                            unit(j, g, i)

            def dense():
                steps(NT, 0)
                turned((NT * STEPS - 1) % 3, NT * STEPS - 1)

            def experts(rnd):
                n0 = rnd * (EXPERTS + 1)

                def picked(n):
                    for half in range(2):
                        act.wait_ge(s_gather, 2 * n + (half + 1))
                        for q in range(4):
                            c = 4 * half + q
                            last = A(xeT[:, c, :], ps[:, 6 + half, q * P:(q + 1) * P], ACT.Copy,
                                     scale=param(1, "ln_ffn")[:, c:c + 1])
                        last.then_inc(s_xeT, 1)

                picked(n0)
                with act.Fori(0, EXPERTS) as e:
                    ex = e + rnd * EXPERTS
                    ue = NT * STEPS + ex * STEPS
                    steps(1, ue)
                    picked(n0 + e + 1)
                    turned((STEPS - 1) % 3, ue + STEPS - 1)
                    act.wait_ge(s_spt, ex + 2)
                    A(spillT[:], ps[:, 3, 0:T], ACT.Copy).then_inc(s_sptc, 1)
                    act.wait_ge(s_down, ue + STEPS)
                    act.wait_ge(s_scat, 4 * ex + 1)
                    A(ye[:, 0, :], ps[:, 4, :], ACT.Copy).then_inc(s_ye, 1)
                    A(ye[:, 1, :], ps[:, 5, :], ACT.Copy).then_inc(s_ye, 1)

            act.nop().then_inc(s_ye, 1)
            act.wait_ge(s_in, INPUTS * 16)
            mixer(0)
            dense()
            mixer(1)
            act.wait_ge(s_m1, 2)
            A(rwork[:, 1, :, :], rwork[:, 0, :, :], ACT.Exp).then_inc(s_rexp, 1)
            act.wait_ge(s_over, 1)
            experts(0)
            more = act.value_load(over[0:1, 0:1], min_val=0, max_val=1)
            with act.If(more > 0):
                experts(1)
            act.wait_ge(s_last, 1)
            rms_squares(2 * DEPTH)

        @block.vector
        def _(dve):
            V = nc.vector
            made = [0]

            def link(ins):
                made[0] += 1
                ins.then_inc(v_done, 1)
                dve.wait_ge(v_done, made[0])

            def rms_apply(n, gain=None):
                dve.wait_ge(s_ss, NT * (n + 1))
                V.tensor_scalar(stat[:, 1, :], stat[:, 0, :], 1.0 / D, EPS, ALU.mult, ALU.add).then_inc(s_ms, 1)
                dve.wait_ge(s_root, n + 1)
                link(V.reciprocal(stat[:, 3, :], stat[:, 2, :]))
                if gain is None:
                    for i in range(NT):
                        V.tensor_scalar(xn[:, i, :], x[:, i, :], stat[:, 3, i:i + 1], None, ALU.mult)\
                            .then_inc(s_xn, 1)
                else:
                    for i in range(NT):
                        V.scalar_tensor_tensor(out=res[:, i, :], in0=x[:, i, :], scalar=stat[:, 3, i:i + 1],
                                               in1=gain, op0=ALU.mult, op1=ALU.mult).then_inc(s_res, 1)

            def conv_part(l, part):
                w = param(l, "conv_w").rearrange("p (c k) -> p c k", c=NC)
                b = param(l, "conv_b")
                taps = range(part * CONV_K // CONV_PARTS, (part + 1) * CONV_K // CONV_PARTS)
                for k in taps:
                    for c in range(NC):
                        win = hc[:, c, k:k + T]
                        o = cacc[:, (CONV_K - 1 - k) % 2, c, :]
                        if k == 0:
                            ins = V.tensor_scalar(o, win, w[:, c, 0:1], b[:, c:c + 1], ALU.mult, ALU.add)
                        else:
                            ins = V.scalar_tensor_tensor(out=o, in0=win, scalar=w[:, c, k:k + 1],
                                                         in1=cacc[:, (CONV_K - k) % 2, c, :], op0=ALU.mult,
                                                         op1=ALU.add)
                    if k == CONV_K - 1:
                        ins.then_inc(s_conv, 1)
                    else:
                        link(ins)

            def mixer(l):
                for stage, k in MIXER:
                    if stage == "norm":
                        rms_apply(2 * l + k)
                        gain = param(l, "ln_attn" if k == 0 else "ln_ffn")
                        for q in range(4):
                            i, half = divmod(q, 2)
                            full(dve, l, stage, k, q)
                            is_free(V.tensor_tensor(hT[:, 4 * half:4 * half + 4, i * P:(i + 1) * P],
                                                    bank(l, stage, k, q).rearrange("p (c t) -> p c t", c=4),
                                                    spread(gain[:, 4 * half:4 * half + 4], 2, P), ALU.mult),
                                    l, stage, k, q)
                    elif stage == "ks":
                        full(dve, l, stage)
                        is_free(V.tensor_copy(kT[:], bank(l, stage).rearrange("p (c t) -> p c t", c=2)), l, stage)
                    elif stage == "kcv":
                        full(dve, l, stage)
                        src = bank(l, stage).rearrange("p (v c j r) -> p v j c r", v=2, c=CB, j=8, r=2)
                        pe_ = param(l, "pe").rearrange("p (v h j) -> p v h j", v=2, h=2)
                        for g in range(2):
                            for r in range(2):
                                for hi in range(2):
                                    lo = r * HD
                                    for v in range(2):
                                        last = V.tensor_tensor(
                                            blocks[lo:lo + HD, v, hi, :, g, 0:NBLK],
                                            src[g * HD:(g + 1) * HD, v, :, hi:hi + NBLK, r],
                                            spread(pe_[lo:lo + HD, v, hi, :], 2, NBLK), ALU.add)
                        is_free(last, l, stage)
                    elif stage == "ca":
                        full(dve, l, stage)
                        freed(dve, l, "cg")
                        is_free(V.tensor_tensor(hc[:, :, CONV_K - 1:], bank(l, stage).rearrange("p (c t) -> p c t", c=NC),
                                                sig[:], ALU.mult), l, stage)
                        freed(dve, l, "ca")
                    elif stage == "conv":
                        conv_part(l, k)
                    elif stage == "score":
                        br, g, i, c0, n = UNITS[k]
                        full(dve, l, stage, k)
                        keys = (i + 1) * P
                        link(V.tensor_reduce(amax[:, k, 0:n], bank(l, stage, k).rearrange("p (n k) -> p n k", n=n),
                                             AX.X, ALU.max))
                        V.tensor_scalar(nmax[:, k, 0:n], amax[:, k, 0:n], -SCALE, None, ALU.mult)\
                            .then_inc(s_amax, 1)
                    elif stage == "pv":
                        br, g, i, c0, n = UNITS[k]
                        dve.wait_ge(s_exp, l * len(UNITS) + k + 1)
                        link(V.reciprocal(arec[:, k, 0:n], asum[:, k, 0:n]))
                        if k == 0:
                            freed(dve, l, "gl")
                        h0 = g * HPG + c0
                        link(V.tensor_tensor(awgt[:, k, 0:n], arec[:, k, 0:n], gates[:, i, h0:h0 + n, 1 + br],
                                             ALU.mult))
                        full(dve, l, stage, k)
                        is_free(V.tensor_tensor(obr[:, br, i, h0:h0 + n, :],
                                                bank(l, stage, k)[:, 0:n * HD].rearrange("p (n d) -> p n d", n=n),
                                                spread(awgt[:, k, 0:n], 2, HD), ALU.mult), l, stage, k)
                    elif stage == "rqk":
                        full(dve, l, stage, k)
                        o = bank(l, stage, k).rearrange("p (h s d) -> p h s d", h=8, s=2)
                        oh = bank(l, stage, k).rearrange("p (h d) -> p h d", h=8)
                        cos = const("cos").rearrange("p (i d) -> p i d", i=NT)[:, k, :]
                        sin = const("sin").rearrange("p (i s d) -> p i s d", i=NT, s=2)[:, k, :, :]
                        V.tensor_tensor(rot[:, 0, :, :], oh, spread(cos, 1, 8), ALU.mult)
                        r1 = rot[:, 1, :, :].rearrange("p h (s d) -> p h s d", s=2)
                        V.tensor_tensor(r1[:, :, 0, :], o[:, :, 1, :], spread(sin[:, 0, :], 1, 8), ALU.mult)
                        link(V.tensor_tensor(r1[:, :, 1, :], o[:, :, 0, :], spread(sin[:, 1, :], 1, 8), ALU.mult))
                        is_free(V.tensor_tensor(rqk[:, k, :, :], rot[:, 0, :, :], rot[:, 1, :, :], ALU.add),
                                l, stage, k)
                        freed(dve, l, stage, k)
                    elif stage == "cmpkv":
                        full(dve, l, stage)
                        o = bank(l, stage)
                        V.tensor_copy(kc[:], o[:, 0:2 * CB])
                        is_free(V.tensor_tensor(vblk[:], spread(o[:, HD:2 * HD], 1, HEADS),
                                                spread(const("head_block"), 2, HD), ALU.mult), l, stage)
                    elif stage == "cscore":
                        add = const("cmp_add").rearrange("p (i c) -> p i c", i=NT)
                        keep = const("cmp_keep").rearrange("p (i c) -> p i c", i=NT)
                        for g in range(2):
                            full(dve, l, stage, 0, g)
                            o = bank(l, stage, 0, g)[:, 0:NT * HPG * CB].rearrange("p (i h c) -> p i h c", i=NT, h=HPG)
                            for i in range(NT):
                                last = V.scalar_tensor_tensor(out=cs[:, i, g * HPG:(g + 1) * HPG, :], in0=o[:, i, :, :],
                                                              scalar=SCALE, in1=spread(add[:, i, :], 1, HPG),
                                                              op0=ALU.mult, op1=ALU.add)
                            is_free(last, l, stage, 0, g)
                        freed(dve, l, stage, 0, 1)
                        c3 = cs[:].rearrange("p i h c -> p (i h) c")
                        st = cstat[:].rearrange("p s i h -> p s (i h)")
                        link(V.tensor_reduce(st[:, 0, :], c3, AX.X, ALU.max))
                        V.tensor_tensor(cs2[:].rearrange("p i h c -> p (i h) c"), c3, spread(st[:, 0, :], 2, CB),
                                        ALU.subtract).then_inc(s_cs2, 1)
                        dve.wait_ge(s_cexp, l + 1)
                        link(V.tensor_reduce(st[:, 1, :], c3, AX.X, ALU.add))
                        link(V.reciprocal(st[:, 2, :], st[:, 1, :]))
                        V.tensor_tensor(cstat[:, 3, :, :], cstat[:, 2, :, :], gates[:, :, :, 0], ALU.mult)
                        for i in range(NT):
                            last = V.tensor_tensor(cs2[:, i, :, :], cs[:, i, :, :], spread(keep[:, i, :], 1, HEADS),
                                                   ALU.mult)
                        link(last)
                        V.tensor_tensor(cprob[:].rearrange("p i h c -> p (i h) c"),
                                        cs2[:].rearrange("p i h c -> p (i h) c"), spread(st[:, 3, :], 2, CB),
                                        ALU.mult).then_inc(s_cprob, 1)
                    elif stage == "rets":
                        b, t = k % 2, k // 2
                        full(dve, l, stage, k)
                        n = T - t * P
                        dec = const("decay").rearrange("p (u b t) -> p u b t", u=2, b=2)[:, :, b, 0:n]
                        dst = (rp0 if t == 0 else rp1)[:].rearrange("p (u b) t -> p u b t", b=2)[:, :, b, :]
                        is_free(V.tensor_tensor(dst, bank(l, stage, k)[:, 0:2 * n].rearrange("p (u t) -> p u t", u=2),
                                                dec, ALU.mult), l, stage, k)
                    elif stage == "reto":
                        full(dve, l, stage)
                        o = bank(l, stage).rearrange("p (i h d) -> p i h d", i=NT, h=RET_HEADS)
                        is_free(V.tensor_copy(ro[:], o), l, stage)
                        freed(dve, l, stage)
                    elif stage == "retnorm":
                        r3 = ro[:].rearrange("p i h d -> p (i h) d")
                        q3 = rsq[:].rearrange("p i h d -> p (i h) d")
                        st = rst[:].rearrange("p s i h -> p s (i h)")
                        link(V.tensor_reduce(st[:, 0, :], r3, AX.X, ALU.add))
                        link(V.tensor_scalar(st[:, 1, :], st[:, 0, :], 1.0 / HD, None, ALU.mult))
                        link(V.tensor_tensor(r3, r3, spread(st[:, 1, :], 2, HD), ALU.subtract))
                        link(V.tensor_tensor(q3, r3, r3, ALU.mult))
                        link(V.tensor_reduce(st[:, 0, :], q3, AX.X, ALU.add))
                        V.tensor_scalar(st[:, 2, :], st[:, 0, :], 1.0 / HD, LN_EPS, ALU.mult, ALU.add)\
                            .then_inc(s_rvar, 1)
                        gn = param(l, "ret_gn").rearrange("p (h d) -> p h d", h=RET_HEADS)
                        freed(dve, l, "rvg", 0)
                        freed(dve, l, "rvg", 1)
                        for i in range(NT):
                            last = V.tensor_tensor(rsq[:, i, :, :], rgate[:, i, :, :], gn, ALU.mult)
                        dve.wait_ge(s_rroot, l + 1)
                        link(V.reciprocal(st[:, 4, :], st[:, 3, :]))
                        link(V.tensor_tensor(r3, r3, spread(st[:, 4, :], 2, HD), ALU.mult))
                        V.tensor_tensor(r3, r3, q3, ALU.mult).then_inc(s_ret, 1)
                    elif stage == "convT":
                        full(dve, l, stage)
                        link(V.tensor_reduce(clst[:, 0, :], bank(l, stage).rearrange("p (i c) -> p i c", i=NT), AX.X,
                                             ALU.add))
                        link(V.tensor_scalar(clst[:, 1, :], clst[:, 0, :], 1.0 / CONV_CH, None, ALU.mult))
                        is_free(V.tensor_tensor(cln[:], bank(l, stage).rearrange("p (i c) -> p i c", i=NT),
                                                spread(clst[:, 1, :], 2, CONV_CH), ALU.subtract), l, stage)
                        freed(dve, l, stage)
                        link(V.tensor_tensor(csq[:], cln[:], cln[:], ALU.mult))
                        link(V.tensor_reduce(clst[:, 0, :], csq[:], AX.X, ALU.add))
                        V.tensor_scalar(clst[:, 2, :], clst[:, 0, :], 1.0 / CONV_CH, LN_EPS, ALU.mult, ALU.add)\
                            .then_inc(s_cvar, 1)
                        dve.wait_ge(s_croot, l + 1)
                        link(V.reciprocal(clst[:, 4, :], clst[:, 3, :]))
                        V.tensor_tensor(cln[:], cln[:], spread(clst[:, 4, :], 2, CONV_CH), ALU.mult)\
                            .then_inc(s_cln, 1)
                    elif stage == "attn_sum":
                        freed(dve, l, "cpv", k)
                        for u in (1, 2, 4, 5, 7, 8, 10, 11) if k else (0, 3, 6, 9):
                            freed(dve, l, "pv", u)
                        link(V.tensor_tensor(obr[:, 1, k, :, :], obr[:, 1, k, :, :], obr[:, 2, k, :, :], ALU.add))
                        V.tensor_tensor(obr[:, 0, k, :, :], obr[:, 0, k, :, :], obr[:, 1, k, :, :], ALU.add)\
                            .then_inc(s_osum, 1)
                    elif stage == "out":
                        for i in range(NT):
                            full(dve, l, stage, k, i)
                            xs = x[:, i, k * 512:(k + 1) * 512]
                            is_free(V.tensor_tensor(xs, bank(l, stage, k, i), xs, ALU.add), l, stage, k, i)

            def steps(tiles, u0):
                def unit(j, g, i):
                    v = j * tiles + i
                    u = u0 + v + g * (SLOTS * tiles)
                    if not isinstance(u, int) or u > 1:
                        dve.wait_ge(s_gtp, u - 1)
                    dve.wait_ge(s_silu, u + 1)
                    V.tensor_tensor(gated[:, v % 3, :], ps[:, v % 3, FC:2 * FC], silu[:, v % 3, :], ALU.mult)\
                        .then_inc(s_gated, 1)

                for j in range(2):
                    for i in range(tiles):
                        unit(j, 0, i)
                with dve.Fori(0, (STEPS - 2) // SLOTS) as g:
                    for j in range(2, 2 + SLOTS):
                        for i in range(tiles):
                            unit(j, g, i)

            def dense():
                steps(NT, 0)
                dve.wait_ge(s_down, NT * STEPS)
                for i in range(NT):
                    for n in range(2):
                        xs = x[:, i, n * 512:(n + 1) * 512]
                        V.tensor_tensor(xs, ps[:, 4 + 2 * i + n, :], xs, ALU.add).then_inc(s_dense, 1)

            def routing():
                dve.wait_ge(s_logit, 1)
                lg = logit
                V.memset(sel[:], 0.0)
                V.memset(gate[:], 0.0)
                link(V.tensor_copy(lg[:], ps[:, 0, 0:NT * EXPERTS].rearrange("p (i e) -> p i e", i=NT)))
                tie = const("earlier").rearrange("p (e f) -> p e f", e=EXPERTS)
                for i in range(NT):
                    mine, other = spread(lg[:, i, :], 2, EXPERTS), spread(lg[:, i, :], 1, EXPERTS)
                    V.tensor_tensor(rcmp[:, 0, i, :, :], other, mine, ALU.is_gt)
                    link(V.tensor_tensor(rcmp[:, 1, i, :, :], other, mine, ALU.is_equal))
                    link(V.tensor_tensor(rcmp[:, 2, i, :, :], rcmp[:, 1, i, :, :], tie, ALU.mult))
                    link(V.tensor_tensor(rcmp[:, 0, i, :, :], rcmp[:, 0, i, :, :], rcmp[:, 2, i, :, :], ALU.add))
                link(V.tensor_reduce(rwork[:, 3, :, :], rcmp[:, 0, :, :, :], AX.X, ALU.add))
                link(V.tensor_reduce(rmax[:, 0, :], lg[:], AX.X, ALU.max))
                V.tensor_scalar(sel[:, :, 0:EXPERTS], rwork[:, 3, :, :], 1.5, None, ALU.is_lt).then_inc(s_sel, 1)
                for i in range(NT):
                    V.tensor_scalar(rwork[:, 0, i, :], lg[:, i, :], rmax[:, 0, i:i + 1], None, ALU.subtract)\
                        .then_inc(s_m1, 1)
                dve.wait_ge(s_sel, 1)
                dve.wait_ge(s_rexp, 1)
                link(V.tensor_tensor(rwork[:, 2, :, :], rwork[:, 1, :, :], sel[:, :, 0:EXPERTS], ALU.mult))
                link(V.tensor_reduce(rmax[:, 1, :], rwork[:, 2, :, :], AX.X, ALU.add))
                link(V.reciprocal(rmax[:, 0, :], rmax[:, 1, :]))
                link(V.tensor_tensor(gate[:, :, 0:EXPERTS], rwork[:, 2, :, :], spread(rmax[:, 0, :], 2, EXPERTS),
                                     ALU.mult))
                dve.wait_ge(s_rankp, 1)
                n = EXPERTS + 1
                V.tensor_copy(rank[:], ps[:, 1, 0:2 * n].rearrange("p (i e) -> p i e", i=NT))
                link(V.tensor_reduce(cmx[:], ps[:, 1, 2 * n:2 * n + EXPERTS], AX.X, ALU.max))
                V.tensor_scalar(over[:], cmx[:], P + 0.5, None, ALU.is_gt).then_inc(s_over, 1)
                dve.wait_ge(s_over, 1)

            def experts(rnd):
                n0 = rnd * (EXPERTS + 1)
                slots = const("slot").rearrange("p (r s) -> p r s", r=NT)[:, rnd, :]

                def picks(dst, by, e, done):
                    for i in range(NT):
                        last = V.tensor_scalar(dst[:, i, :], slots, rank[:, i, bass.ds(e, 1)], by[:, i, bass.ds(e, 1)],
                                               ALU.is_equal, ALU.mult)
                    last.then_inc(done, 1)

                if rnd:
                    dve.wait_ge(s_gather, 2 * n0)
                picks(pick, sel, 0, s_pick)
                with dve.Fori(0, EXPERTS) as e:
                    ex = e + rnd * EXPERTS
                    dve.wait_ge(s_gather, 2 * (n0 + e) + 2)
                    picks(pick, sel, e + 1, s_pick)
                    dve.wait_ge(s_spt, ex + 1)
                    picks(spill, gate, e, s_spill)
                    steps(1, NT * STEPS + ex * STEPS)
                    for i in range(NT):
                        for n in range(2):
                            dve.wait_ge(s_scat, 4 * ex + (2 * i + n + 2))
                            xs = x[:, i, n * 512:(n + 1) * 512]
                            V.tensor_tensor(xs, ps[:, 6 + n, :], xs, ALU.add).then_inc(s_xadd, 1)
                dve.wait_ge(s_xadd, 4 * EXPERTS * (rnd + 1) + 1)

            dve.nop().then_inc(s_xadd, 1)
            V.memset(hc[:], 0.0)
            link(V.memset(blocks[:], 0.0))
            dve.wait_ge(s_in, INPUTS * 16)
            mixer(0)
            dense()
            mixer(1)
            routing()
            experts(0)
            more = dve.value_load(over[0:1, 0:1], min_val=0, max_val=1)
            with dve.If(more > 0):
                experts(1)
            dve.nop().then_inc(s_last, 1)
            rms_apply(2 * DEPTH, gain=gfin[:])

        @block.gpsimd
        def _(pool):
            pass


def _constants():
    c = np.zeros((P, CONST_COLS), np.float32)

    def put(name, v):
        a, n = CONSTS[name]
        c[:, a:a + n] = np.asarray(v, np.float32).reshape(P, n)

    p = np.arange(P)
    put("ident", np.eye(P))
    put("causal", np.where(p[None, :] <= p[:, None], 0.0, NEG))
    tok = p[:, None, None] + P * np.arange(NT)[None, :, None]
    blk = np.arange(CB)[None, None, :]
    seen = (blk * CMP_STRIDE + CMP_LEN - 1 <= tok) & (blk < NBLK)
    put("cmp_add", np.where(seen, 0.0, NEG))
    put("cmp_keep", seen)
    put("head_block", p[:, None] // CB == np.arange(HEADS)[None, :])
    half = HD // 2
    inv = np.float32(10000.0) ** (-np.arange(half, dtype=np.float32) / np.float32(half))
    ang = (tok.astype(np.float32) * inv[None, None, :]).astype(np.float32)
    put("cos", np.concatenate([np.cos(ang), np.cos(ang)], -1))
    put("sin", np.concatenate([-np.sin(ang), np.sin(ang)], -1))
    lg = np.log1p(-np.exp2(-5.0 - np.arange(RET_HEADS)))
    rel = np.arange(T)[None, None, :] - p[:, None, None]
    put("decay", np.where(rel >= 0, np.exp(np.maximum(rel, 0) * lg[None, :, None]) * SCALE, 0.0))
    put("before", p[:, None] < p[None, :])
    put("ones", np.ones((P, P)))
    put("slot", np.broadcast_to(np.arange(NT * P)[None, :], (P, NT * P)))
    e = np.arange(EXPERTS)
    put("earlier", np.broadcast_to((e[None, :] < e[:, None])[None], (P, EXPERTS, EXPERTS)))
    return c


def _by_partition(w, k):
    return w.reshape(k, P, -1).transpose(1, 0, 2)


def _layout(a):
    f = {n: np.asarray(v) for n, v in a.items()}
    q = [np.r_[c * HD:(c + 1) * HD, (4 + c) * HD:(5 + c) * HD] for c in range(HPG)]
    at = lambda s, n: np.arange(s, s + n)
    kc, vc, ks, vs, kw, vw = (at(512 + n * 128, 128) for n in range(6))
    gl, conv = at(1280, 24), at(1304, 512)
    rq, rk, rv, rg = (at(1816 + n * 256, 256) for n in range(4))
    cols = [np.concatenate(q + [ks, kw]), np.concatenate([kc, vc, conv]), np.concatenate([vs, vw, gl, rk]),
            np.concatenate([rq, rv, rg])]
    mix, params = [], []
    for l in range(DEPTH):
        parts = [_by_partition(f["w_in"][l][:, c], KD) for c in cols]
        w1 = [_by_partition(f["cmp_w1"][l, v], 16) for v in range(2)]
        w2 = [_by_partition(f["cmp_w2"][l, v], 2) for v in range(2)]
        pw = _by_partition(f["conv_pw"][l], NC)
        flat = lambda *z: np.concatenate([y.reshape(P, -1) for y in z], axis=1)
        parts.append(flat(w1[0], np.concatenate([w2[0], w2[0]], axis=2)))
        parts.append(flat(w1[1], w2[1], pw))
        wo = _by_partition(f["w_out"][l], KD)
        parts += [wo[:, :, :512], wo[:, :, 512:]]
        mix.append(np.concatenate([np.ascontiguousarray(z).reshape(-1) for z in parts]))
        wide = lambda v: v.reshape(-1, P).T
        pe = f["cmp_pe"][l].reshape(2, 16, P).transpose(2, 0, 1).reshape(P, 32)
        cw = f["conv_w"][l].T.reshape(NC, P, CONV_K).transpose(1, 0, 2).reshape(P, -1)
        params.append(np.concatenate([
            wide(f["ln_attn"][l]), wide(f["ln_ffn"][l]), pe, cw, wide(f["conv_b"][l]), wide(f["conv_ln_g"][l]),
            wide(f["conv_ln_b"][l]), np.broadcast_to(f["ret_gn"][l][None], (P, RET_HEADS * HD))], axis=1))

    def ffn(w13, w2):
        n = w13.shape[0]
        up = w13.reshape(n, KD, P, 2, STEPS, FC).transpose(0, 4, 2, 1, 3, 5).reshape(n, STEPS, P, -1)
        down = w2.reshape(n, STEPS, FC // P, P, D).transpose(0, 1, 3, 2, 4).reshape(n, STEPS, P, -1)
        return np.concatenate([up, down], axis=3).reshape(n * STEPS, P, FFN_ITEM)

    c = np.ascontiguousarray
    return {
        "x_in": c(f["x"].reshape(T, D)), "consts_in": _constants(), "params_in": c(np.stack(params, axis=1)),
        "mix_in": c(np.stack(mix)), "ffn_in": ffn(f["ffn_w13"], f["ffn_w2"]), "moe_in": ffn(f["moe_w13"][0], f["moe_w2"][0]),
        "router_in": c(_by_partition(f["router"][0], KD)), "final_in": c(np.broadcast_to(f["ln_final"][None], (P, D))),
    }


_ORDER = ["x_in", "consts_in", "params_in", "mix_in", "ffn_in", "moe_in", "router_in", "final_in"]


def kernel(**inputs):
    import concourse.bacc as _bacc
    from concourse.bass_utils import run_bass_kernel_spmd as _run

    nc = _bacc.Bacc("TRN2", target_bir_lowering=False, num_devices=1)
    arrays = _layout(inputs)
    args = [nc.dram_tensor(n, arrays[n].shape, F32, kind="ExternalInput").ap() for n in _ORDER]
    args.append(nc.dram_tensor("out_0", (T, D), F32, kind="ExternalOutput").ap())
    hybrid_trunk_kernel(nc, *args)
    r = _run(nc, [arrays], core_ids=[0])
    return r.results[0]["out_0"].reshape(1, T, D)
```

```python
from contextlib import ExitStack

import numpy as np

import concourse.bass as bass
from concourse import mybir

F32 = mybir.dt.float32
F32R = mybir.dt.float32r
BF16 = mybir.dt.bfloat16
I32 = mybir.dt.int32
ALU = mybir.AluOpType
ACT = mybir.ActivationFunctionType
AX = mybir.AxisListType

P = 128
D = 1024
T = 256
NT = T // P
KD = D // P
DEPTH = 2
HD = 64
HEADS = 8
HPG = 4
CMP_STRIDE, CMP_LEN, CMP_HID = 16, 32, 256
NBLK = T // CMP_STRIDE - CMP_LEN // CMP_STRIDE + 1
CB = 16
CONV_CH, CONV_K = 256, 31
NC = CONV_CH // P
RET_HEADS = 4
D_FF = 2816
FC = 256
STEPS = D_FF // FC
EXPERTS = 8
SCALE = HD ** -0.5
NEG = -1e30
EPS, LN_EPS = 1e-6, 1e-5
FFN_WORDS = 4832
ARENA = 22330

SLOTS = 3
SLOT = 6144
FFN_ITEM = KD * 2 * FC + (FC // P) * D
MIX_ITEMS = (KD * 768, KD * 768, KD * 536, KD * 768, 16 * CMP_HID + 2 * P, 16 * CMP_HID + 2 * HD + 2 * CONV_CH,
             KD * 512, KD * 512)
MIX_OFF = [sum(MIX_ITEMS[:n]) * P for n in range(len(MIX_ITEMS) + 1)]
MIX_FILLS = [len([m for m in range(len(MIX_ITEMS)) if m % SLOTS == s]) for s in range(SLOTS)]
FFN_FILLS = [len([m for m in range(STEPS) if m % SLOTS == s]) for s in range(SLOTS)]

CONSTS = {}
CONST_COLS = 0
for _name, _n in (("ident", P), ("causal", P), ("cmp_add", NT * CB), ("cmp_keep", NT * CB), ("head_block", HEADS),
                  ("cos", NT * HD), ("sin", NT * HD), ("decay", RET_HEADS * T), ("before", P), ("ones", P),
                  ("slot", NT * P), ("earlier", EXPERTS * EXPERTS)):
    CONSTS[_name] = (CONST_COLS, _n)
    CONST_COLS += _n

EARLY = 2 * P

PARAMS = {}
PARAM_COLS = 0
for _name, _n in (("ln_attn", KD), ("ln_ffn", KD), ("pe", 2 * 16), ("conv_w", NC * CONV_K), ("conv_b", NC),
                  ("conv_g", NC), ("conv_beta", NC), ("ret_gn", RET_HEADS * HD)):
    PARAMS[_name] = (PARAM_COLS, _n)
    PARAM_COLS += _n

UNITS = [(br, g, i, c, n) for br in range(2) for g in range(2) for i, c, n in ((0, 0, 4), (1, 0, 2), (1, 2, 2))]

CONV_PARTS = 8
MIXER = [
    ("norm", 0), ("q", 0), ("q", 1), ("ks", 0), ("score", 0), ("kcv", 0), ("score", 1), ("probT", 0), ("vsw", 0),
    ("score", 2), ("gl", 0), ("probT", 1), ("pv", 0), ("cg", 0), ("score", 3), ("probT", 2), ("pv", 1), ("ca", 0),
    ("conv", 0), ("score", 4), ("probT", 3), ("pv", 2), ("rqk", 0), ("conv", 1), ("score", 5), ("probT", 4),
    ("pv", 3), ("rqk", 1), ("conv", 2), ("score", 6), ("probT", 5), ("pv", 4), ("hid", 0), ("conv", 3), ("retT", 0),
    ("score", 7), ("probT", 6), ("pv", 5), ("hid", 1), ("conv", 4), ("retT", 1), ("hidT", 0), ("score", 8),
    ("probT", 7), ("pv", 6), ("rvg", 0), ("conv", 5), ("hidT", 1), ("rets", 0), ("rets", 1), ("score", 9),
    ("probT", 8), ("pv", 7), ("cmpkv", 0), ("conv", 6), ("cscore", 0), ("score", 10), ("rvg", 1), ("probT", 9),
    ("pv", 8), ("rets", 2), ("rets", 3), ("score", 11), ("probT", 10), ("pv", 9), ("conv", 7), ("cprobT", 0),
    ("probT", 11), ("pv", 10), ("reto", 0), ("pv", 11), ("cpv", 0), ("cpv", 1), ("attn_sum", 0), ("attn_sum", 1),
    ("convT", 0), ("out", 0), ("retnorm", 0), ("convB", 0), ("out", 1), ("retcat", 0), ("conv_pw", 0),
    ("out_rest", 0), ("out_rest", 1), ("norm", 1)]

PSUM_GROUPS = {"norm": 4, "q": 1, "ks": 1, "score": 1, "kcv": 1, "cg": 1, "ca": 1, "probT": 1, "vsw": 1, "pv": 1,
               "rqk": 1, "rvg": 1, "gl": 1, "hid": 1, "hidT": 1, "cmpkv": 1, "retT": 1, "cscore": 2, "rets": 1,
               "cprobT": 1, "reto": 1, "cpv": 1, "convT": 1, "convB": 1, "attn_sum": 1, "conv_pw": 1, "retcat": 1, "out": 2,
               "conv": 0, "retnorm": 0, "out_rest": 0}
BANKS = 8
SCATTER = ((6, 7), (1, 3))
PIECE = 1024
UP = KD * 2 * FC // PIECE
DOWN = (FC // P) * D // PIECE
PIECES = UP + DOWN
PASS = STEPS * PIECES
LAST_READ = (("ks", 0, 0), ("ca", 0, 0), ("rqk", 1, 0), ("rvg", 1, 0), ("cmpkv", 0, 0), ("conv_pw", 0, 0),
             ("out", 0, 1), ("out", 1, 1))
LAST_STEP = [max(j for j in range(STEPS) if j % SLOTS == s) for s in range(SLOTS)]
LAST_ITEM = [max(m for m in range(len(MIX_ITEMS)) if m % SLOTS == s) for s in range(SLOTS)]
GROUP = {}
_n = 0
for _l in range(DEPTH):
    for _stage, _k in MIXER:
        for _j in range(PSUM_GROUPS[_stage]):
            GROUP[(_l, _stage, _k, _j)] = (_n % BANKS, _n // BANKS + 1)
            _n += 1


def up_at(j, p):
    return p if j == 0 else UP + (j - 1) * PIECES + p


def down_at(j, c):
    return up_at(j + 1, UP if j < STEPS - 1 else 0) + c


def spread(ap, axis, n):
    u = ap.unsqueeze(axis)
    shape = list(u.shape)
    shape[axis] = n
    return u.broadcast_to(shape)


def hybrid_trunk_kernel(nc, x_in, consts_in, params_in, mix_in, ffn_in, moe_in, router_in, final_in, out):
    with ExitStack() as ctx:
        def sb(name, shape, dt=F32):
            return ctx.enter_context(nc.sbuf_tensor(name, shape, dt))

        def sem(name):
            return ctx.enter_context(nc.semaphore(name))

        ps = ctx.enter_context(nc.psum_tensor("ps", [P, BANKS, 512], F32))
        ring = sb("ring", [P, SLOTS, SLOT])
        cst = sb("cst", [P, CONST_COLS])
        par = sb("par", [P, DEPTH, PARAM_COLS])
        router = sb("router", [P, KD, EXPERTS])
        gfin = sb("gfin", [P, D])
        x = sb("x", [P, NT, D])
        xn = sb("xn", [P, NT, D])
        hT_at = nc.sbuf_base
        hT = sb("hT", [P, KD, T])
        stat = sb("stat", [P, 4, NT])

        arena_at = nc.sbuf_base
        arena = sb("arena", [P, ARENA])

        def arena_of():
            at = [0]

            def view(name, shape):
                n = int(np.prod(shape[1:]))
                v = arena[:, at[0]:at[0] + n]
                at[0] += n
                assert at[0] <= ARENA, (name, at[0])
                dims = " ".join(f"a{i}" for i in range(1, len(shape)))
                return v.rearrange(f"p ({dims}) -> p {dims}", **{f"a{i}": shape[i] for i in range(1, len(shape))})
            return view

        mix = arena_of()
        qT = mix("qT", [P, HPG, T])
        kT = mix("kT", [P, 2, 2, T])
        vv = mix("vv", [P, NT, 2, 2, HD])
        gates = mix("gates", [P, NT, HEADS, 3])
        prob = mix("prob", [P, 3, 512])
        probT = mix("probT", [P, 3, 512])
        amax = mix("amax", [P, len(UNITS), HPG])
        nmax = mix("nmax", [P, len(UNITS), HPG])
        asum = mix("asum", [P, len(UNITS), HPG])
        arec = mix("arec", [P, len(UNITS), HPG])
        awgt = mix("awgt", [P, len(UNITS), HPG])
        obr = mix("obr", [P, 3, NT, HEADS, HD])
        catT = mix("catT", [P, KD, T])
        blocks = sb("blocks", [P, 2, 2, 8, 2, CB])
        hid = mix("hid", [P, 2, 2, 2 * CB])
        hidv = mix("hidv", [P, 4, HPG, CB])
        kc = mix("kc", [P, 2 * CB])
        vblk = mix("vblk", [P, HEADS, HD])
        cs = mix("cs", [P, NT, HEADS, CB])
        cs2 = mix("cs2", [P, NT, HEADS, CB])
        cprob = mix("cprob", [P, NT, HEADS, CB])
        cstat = mix("cstat", [P, 4, NT, HEADS])
        cprobT = mix("cprobT", [P, NT, P])
        sig = mix("sig", [P, NC, T])
        hc = sb("hc", [P, NC, CONV_K - 1 + T])
        cacc = mix("cacc", [P, 2, NC, T])
        cln = mix("cln", [P, NT, CONV_CH])
        hrow = cln[0:2 * CB, :, :]
        csq = mix("csq", [P, NT, CONV_CH])
        clst = mix("clst", [P, 5, NT])
        cact = mix("cact", [P, NC, T])
        rqk = mix("rqk", [P, NT, 2 * RET_HEADS, HD])
        rot = mix("rot", [P, 2, 2 * RET_HEADS, HD])
        rT = mix("rT", [P, 4, T])
        rv = mix("rv", [P, NT, RET_HEADS, HD])
        rgate = mix("rgate", [P, NT, RET_HEADS, HD])
        rp0 = mix("rp0", [P, RET_HEADS, T])
        rp1 = mix("rp1", [P, RET_HEADS, P])
        ro = mix("ro", [P, NT, RET_HEADS, HD])
        rsq = rp0[:, 0:2, :].rearrange("p i (h d) -> p i h d", h=RET_HEADS)
        rst = mix("rst", [P, 5, NT, RET_HEADS])

        ffn = arena_of()
        silu = ffn("silu", [P, NT, FC])
        gated = ffn("gated", [P, NT, FC])
        logit = ffn("logit", [P, NT, EXPERTS])
        rcmp = ffn("rcmp", [P, 3, NT, EXPERTS, EXPERTS])
        rwork = ffn("rwork", [P, 4, NT, EXPERTS])
        rmax = ffn("rmax", [P, 2, NT])
        sel = ffn("sel", [P, NT, EXPERTS])
        gate = ffn("gate", [P, NT, EXPERTS])
        rank = ffn("rank", [P, NT, EXPERTS])
        cmx = ffn("cmx", [P, 1])
        over = sb("over", [P, 1], I32)
        identb = sb("identb", [P, P], BF16)
        causalb = sb("causalb", [P, P], BF16)

        at_word = [2 * NT * FC + 544]

        def place(name, shape, dt, words):
            t = nc.alloc_sbuf_tensor_at(name, shape, dt, offset=arena_at + 4 * at_word[0])
            at_word[0] += words
            assert at_word[0] <= FFN_WORDS
            return t

        pick = place("pick", [P, NT, P], BF16, NT * P // 2)
        xb = [nc.alloc_sbuf_tensor_at("xb0", [P, NT, D], BF16, offset=hT_at),
              nc.alloc_sbuf_tensor_at("xb1", [P, NT, D], BF16, offset=hT_at + 2 * NT * D),
              place("xb2", [P, NT, D], BF16, NT * D // 2)]
        yeh, yel = place("yeh", [P, 2, 512], F32R, 1024), place("yel", [P, 2, 512], F32R, 1024)

        split_at = [FFN_WORDS]

        def split(name, shape):
            n = int(np.prod(shape[1:]))
            t = nc.alloc_sbuf_tensor_at(name, shape, F32R, offset=arena_at + 4 * split_at[0])
            split_at[0] += n
            assert split_at[0] <= ARENA
            return t

        wh, wl = split("wh", [P, PIECES, PIECE]), split("wl", [P, PIECES, PIECE])
        hTh, hTl = split("hTh", [P, KD, T]), split("hTl", [P, KD, T])
        gTh, gTl = split("gTh", [P, NT, FC // P, P]), split("gTl", [P, NT, FC // P, P])
        pickT = gTh[:, 1, :, :]
        res = xn

        bank_full = [sem(f"bank_full{b}") for b in range(BANKS)]
        bank_free = [sem(f"bank_free{b}") for b in range(BANKS)]
        slot_full = [sem(f"slot_full{s}") for s in range(SLOTS)]
        down_full = [sem(f"down_full{s}") for s in range(SLOTS)]
        s_in = sem("s_in")
        s_late = sem("s_late")
        s_const = sem("s_const")
        s_x = sem("s_x")
        s_ss = sem("s_ss")
        s_ms = sem("s_ms")
        s_root = sem("s_root")
        s_xn = sem("s_xn")
        s_amax = sem("s_amax")
        s_exp = sem("s_exp")
        s_cs2 = sem("s_cs2")
        s_cexp = sem("s_cexp")
        s_cprob = sem("s_cprob")
        s_conv = sem("s_conv")
        s_cvar = sem("s_cvar")
        s_croot = sem("s_croot")
        s_cln = sem("s_cln")
        s_rvar = sem("s_rvar")
        s_rroot = sem("s_rroot")
        s_ret = sem("s_ret")
        s_osum = sem("s_osum")
        v_done = sem("v_done")
        s_zero = sem("s_zero")
        s_hTh = sem("s_hTh")
        s_hTl = sem("s_hTl")
        s_hi = sem("s_hi")
        s_lo = sem("s_lo")
        s_piece = sem("s_piece")
        s_silu = sem("s_silu")
        s_gated = sem("s_gated")
        s_gtp = sem("s_gtp")
        s_gTh = sem("s_gTh")
        s_gTl = sem("s_gTl")
        s_dense = sem("s_dense")
        s_logit = sem("s_logit")
        s_m1 = sem("s_m1")
        s_rexp = sem("s_rexp")
        s_sel = sem("s_sel")
        s_rankp = sem("s_rankp")
        s_over = sem("s_over")
        s_pick = sem("s_pick")
        s_xb = sem("s_xb")
        s_xr = sem("s_xr")
        s_xb2 = sem("s_xb2")
        s_gather = sem("s_gather")
        s_xeh = sem("s_xeh")
        s_xel = sem("s_xel")
        s_spt = sem("s_spt")
        s_sptc = sem("s_sptc")
        s_yeh = sem("s_yeh")
        s_yel = sem("s_yel")
        s_scat = sem("s_scat")
        s_xadd = sem("s_xadd")
        s_last = sem("s_last")
        s_res = sem("s_res")
        s_out = sem("s_out")

        def const(name, n=None):
            a, w = CONSTS[name]
            return cst[:, a:a + (n or w)]

        def param(l, name):
            a, w = PARAMS[name]
            return par[:, l, a:a + w]

        ident = const("ident")
        INPUTS = 2

        def bank(l, stage, k=0, j=0):
            return ps[:, GROUP[(l, stage, k, j)][0], :]

        def full(eng, l, stage, k=0, j=0):
            b, n = GROUP[(l, stage, k, j)]
            eng.wait_ge(bank_full[b], n)

        def freed(eng, l, stage, k=0, j=0):
            b, n = GROUP[(l, stage, k, j)]
            eng.wait_ge(bank_free[b], n)

        def is_full(ins, l, stage, k=0, j=0):
            ins.then_inc(bank_full[GROUP[(l, stage, k, j)][0]], 1)

        def is_free(ins, l, stage, k=0, j=0):
            ins.then_inc(bank_free[GROUP[(l, stage, k, j)][0]], 1)

        def mix_fill(l, m):
            s = m % SLOTS
            return l * (MIX_FILLS[s] + FFN_FILLS[s]) + m // SLOTS + 1

        def item(m):
            return ring[:, m % SLOTS, 0:MIX_ITEMS[m]]

        block = ctx.enter_context(nc.Block())

        @block.sync
        def _(sp):
            sp.dma_start(x[:], x_in.rearrange("(i p) d -> p i d", p=P)).then_inc(s_x, 16)
            sp.dma_start(cst[:, 0:EARLY], consts_in[:, 0:EARLY]).then_inc(s_in, 16)
            sp.dma_start(par[:], params_in).then_inc(s_in, 16)

            def ffn_items(l, q0, src):
                def load(j, last_piece, words, landed):
                    s = j % SLOTS
                    if j >= SLOTS:
                        sp.wait_ge(s_lo, q0 + (last_piece(j - SLOTS) + 1))
                    else:
                        full(sp, l, *LAST_READ[LAST_ITEM[s]])
                        if l:
                            sp.wait_ge(s_lo, q0 - PASS + (last_piece(LAST_STEP[s]) + 1))
                    sp.dma_start(ring[:, s, words], src(j)[:, words]).then_inc(landed[s], 16)

                for j in range(STEPS + 1):
                    if j < STEPS:
                        load(j, lambda i: up_at(i, UP - 1), slice(0, UP * PIECE), slot_full)
                    if j > 0:
                        load(j - 1, lambda i: down_at(i, DOWN - 1), slice(UP * PIECE, FFN_ITEM), down_full)

            for l in range(DEPTH):
                for m, n in enumerate(MIX_ITEMS):
                    s = m % SLOTS
                    if m >= SLOTS:
                        full(sp, l, *LAST_READ[m - SLOTS])
                    elif l:
                        sp.wait_ge(s_lo, down_at(LAST_STEP[s], DOWN - 1) + 1)
                    src = mix_in[l, MIX_OFF[m]:MIX_OFF[m + 1]].rearrange("(p n) -> p n", p=P)
                    sp.dma_start(item(m), src).then_inc(slot_full[s], 16)
                    if l == 0 and m == 0:
                        sp.dma_start(cst[:, EARLY:], consts_in[:, EARLY:]).then_inc(s_const, 16)
                    if l == 0 and m == 1:
                        sp.dma_start(router[:], router_in).then_inc(s_late, 16)
                        sp.dma_start(gfin[:], final_in).then_inc(s_late, 16)
                if l == 0:
                    ffn_items(0, 0, lambda j: ffn_in[j])
                else:
                    with sp.Fori(0, EXPERTS) as e:
                        ffn_items(1, PASS + e * PASS, lambda j: moe_in[e * STEPS + j])
            sp.wait_ge(s_over, 1)
            more = sp.value_load(over[0:1, 0:1], min_val=0, max_val=1)
            with sp.If(more > 0):
                with sp.Fori(0, EXPERTS) as e:
                    ffn_items(1, PASS + (EXPERTS + e) * PASS, lambda j: moe_in[e * STEPS + j])
            for i in range(NT):
                sp.wait_ge(s_res, i + 1)
                sp.dma_start(out[i * P:(i + 1) * P, :], res[:, i, :]).then_inc(s_out, 16)
            sp.wait_ge(s_out, NT * 16)

        @block.tensor
        def _(pe):
            def mm(o, lhsT, rhs, first, last):
                return nc.tensor.matmul(o, lhsT, rhs, start=first, stop=last, skip_group_check=True)

            def flip(o, a):
                return nc.tensor.transpose(o, a, ident)

            def begin(l, stage, k=0, j=0):
                b, n = GROUP[(l, stage, k, j)]
                if n > 1:
                    pe.wait_ge(bank_free[b], n - 1)
                return ps[:, b, :]

            def landed(l, m):
                pe.wait_ge(slot_full[m % SLOTS], 16 * mix_fill(l, m))

            def width_major(o, m, width, col):
                w = item(m).rearrange("p (k n) -> p k n", k=KD)
                for k in range(KD):
                    last = mm(o, w[:, k, col:col + P], hT[:, k, :], k == 0, k == KD - 1)
                return last

            def token_major(o, m, i, col, n):
                w = item(m).rearrange("p (k n) -> p k n", k=KD)
                for k in range(KD):
                    last = mm(o, hT[:, k, i * P:(i + 1) * P], w[:, k, col:col + n], k == 0, k == KD - 1)
                return last

            def mixer(l):
                for stage, k in MIXER:
                    if stage == "norm":
                        for i in range(NT):
                            pe.wait_ge(s_xn, (2 * l + k) * NT + i + 1)
                            for half in range(2):
                                o = begin(l, "norm", k, 2 * i + half)
                                for q in range(4):
                                    c = 4 * half + q
                                    last = flip(o[:, q * P:(q + 1) * P], xn[:, i, c * P:(c + 1) * P])
                                is_full(last, l, "norm", k, 2 * i + half)
                    elif stage == "q":
                        o = begin(l, stage, k)
                        if k == 0:
                            for j in range(4):
                                freed(pe, l, "norm", 0, j)
                            landed(l, 0)
                        width_major(o[:, 0:T], 0, 768, 2 * k * P)
                        is_full(width_major(o[:, T:2 * T], 0, 768, (2 * k + 1) * P), l, stage, k)
                    elif stage == "ks":
                        o = begin(l, stage)
                        width_major(o[:, 0:T], 0, 768, 4 * P)
                        is_full(width_major(o[:, T:2 * T], 0, 768, 5 * P), l, stage)
                    elif stage in ("kcv", "ca", "cg"):
                        o = begin(l, stage)
                        if stage == "kcv":
                            landed(l, 1)
                        col = {"kcv": 0, "ca": 2 * P, "cg": 4 * P}[stage]
                        width_major(o[:, 0:T], 1, 768, col)
                        is_full(width_major(o[:, T:2 * T], 1, 768, col + P), l, stage)
                    elif stage == "vsw":
                        o = begin(l, stage)
                        landed(l, 2)
                        for i in range(NT):
                            last = token_major(o[:, i * 256:(i + 1) * 256], 2, i, 0, 256)
                        is_full(last, l, stage)
                    elif stage == "rqk":
                        o = begin(l, stage, k)
                        if k == 0:
                            landed(l, 3)
                        token_major(o[:, 0:256], 3, k, 0, 256)
                        is_full(token_major(o[:, 256:512], 2, k, 280, 256), l, stage, k)
                    elif stage == "rvg":
                        is_full(token_major(begin(l, stage, k), 3, k, 256, 512), l, stage, k)
                    elif stage == "gl":
                        o = begin(l, stage)
                        for i in range(NT):
                            last = token_major(o[:, i * 24:(i + 1) * 24], 2, i, 256, 24)
                        is_full(last, l, stage)
                    elif stage == "score":
                        br, g, i, c0, n = UNITS[k]
                        keys = (i + 1) * P
                        o = begin(l, stage, k)
                        if k == 0:
                            freed(pe, l, "ks")
                            pe.wait_ge(s_zero, 2 + l)
                            freed(pe, l, "q", 0)
                            freed(pe, l, "q", 1)
                        ov = o[:, 0:n * keys].rearrange("p (n k) -> p n k", n=n)
                        mm(ov[:, :, i * P:keys], identb[:], spread(causalb[:], 1, n), True, False)
                        for c in range(n):
                            last = mm(o[:, c * keys:(c + 1) * keys], qT[:, c0 + c, i * P:(i + 1) * P],
                                      kT[:, g, br, 0:keys], False, c == n - 1)
                        is_full(last, l, stage, k)
                    elif stage == "probT":
                        br, g, i, c0, n = UNITS[k]
                        o = begin(l, stage, k)
                        pe.wait_ge(s_exp, l * len(UNITS) + k + 1)
                        for q in range(4):
                            last = flip(o[:, q * P:(q + 1) * P], prob[:, k % 3, q * P:(q + 1) * P])
                        is_full(last, l, stage, k)
                    elif stage == "pv":
                        br, g, i, c0, n = UNITS[k]
                        o = begin(l, stage, k)
                        freed(pe, l, "probT", k)
                        if k == 0:
                            freed(pe, l, "vsw")
                        for c in range(n):
                            for t in range(i + 1):
                                q = c * (i + 1) + t
                                last = mm(o[:, c * HD:(c + 1) * HD], probT[:, k % 3, q * P:(q + 1) * P],
                                          vv[:, t, br, g, :], t == 0, t == i)
                        is_full(last, l, stage, k)
                    elif stage == "hid":
                        o = begin(l, stage, k)
                        landed(l, 4 + k)
                        if k == 0:
                            freed(pe, l, "kcv")
                        w = item(4 + k)[:, 0:16 * CMP_HID].rearrange("p (j n) -> p j n", j=16)
                        for j in range(16):
                            last = mm(o[0:2 * CB, 0:CMP_HID], blocks[:, k, j // 8, j % 8, :, :], w[:, j, :],
                                      j == 0, j == 15)
                        is_full(last, l, stage, k)
                    elif stage == "hidT":
                        o = begin(l, stage, k)
                        freed(pe, l, "hid", k)
                        for m in range(2):
                            last = nc.tensor.transpose(o[:, m * 32:(m + 1) * 32], hrow[:, k, m * P:(m + 1) * P],
                                                       ident[0:2 * CB, 0:2 * CB])
                        is_full(last, l, stage, k)
                    elif stage == "cmpkv":
                        o = begin(l, stage)
                        freed(pe, l, "hidT", 0)
                        freed(pe, l, "hidT", 1)
                        wk = item(4)[:, 16 * CMP_HID:].rearrange("p (m n) -> p m n", m=2)
                        wv = item(5)[:, 16 * CMP_HID:16 * CMP_HID + 2 * HD].rearrange("p (m n) -> p m n", m=2)
                        for m in range(2):
                            mm(o[:, 0:2 * CB], wk[:, m, :], hid[:, 0, m, :], m == 0, m == 1)
                        for m in range(2):
                            last = mm(o[:, HD:2 * HD], hidv[:, 2 * m:2 * m + 2, :, :], wv[:, m, :], m == 0, m == 1)
                        is_full(last, l, stage)
                    elif stage == "cscore":
                        for g in range(2):
                            o = begin(l, stage, 0, g)
                            if g == 0:
                                freed(pe, l, "cmpkv")
                            lo = g * HD
                            for i in range(NT):
                                for c in range(HPG):
                                    q = i * HPG + c
                                    last = mm(o[:, q * CB:(q + 1) * CB], qT[lo:lo + HD, c, i * P:(i + 1) * P],
                                              kc[lo:lo + HD, g * CB:(g + 1) * CB], True, True)
                            is_full(last, l, stage, 0, g)
                    elif stage == "cprobT":
                        o = begin(l, stage)
                        pe.wait_ge(s_cprob, l + 1)
                        for i in range(NT):
                            last = flip(o[:, i * P:(i + 1) * P], cprob[:, i, :, :].rearrange("p h c -> p (h c)"))
                        is_full(last, l, stage)
                    elif stage == "cpv":
                        o = begin(l, stage, k)
                        if k == 0:
                            freed(pe, l, "cprobT")
                        last = mm(o, cprobT[:, k, :], vblk[:].rearrange("p h d -> p (h d)"), True, True)
                        is_full(last, l, stage, k)
                    elif stage == "retT":
                        o = begin(l, stage, k)
                        freed(pe, l, "rqk", k)
                        for q in range(4):
                            last = flip(o[:, q * P:(q + 1) * P],
                                        rqk[:, k, 2 * q:2 * q + 2, :].rearrange("p h d -> p (h d)"))
                        is_full(last, l, stage, k)
                    elif stage == "rets":
                        b, t = k % 2, k // 2
                        o = begin(l, stage, k)
                        if k == 0:
                            freed(pe, l, "retT", 0)
                            freed(pe, l, "retT", 1)
                        lo, n = b * HD, T - t * P
                        for u in range(2):
                            last = mm(o[:, u * n:(u + 1) * n], rT[lo:lo + HD, 2 + u, t * P:(t + 1) * P],
                                      rT[lo:lo + HD, u, t * P:T], True, True)
                        is_full(last, l, stage, k)
                    elif stage == "reto":
                        o = begin(l, stage)
                        for j in range(4):
                            freed(pe, l, "rets", j)
                        freed(pe, l, "rvg", 0)
                        freed(pe, l, "rvg", 1)
                        for h in range(RET_HEADS):
                            mm(o[:, h * HD:(h + 1) * HD], rp0[:, h, 0:P], rv[:, 0, h, :], True, True)
                        for h in range(RET_HEADS):
                            oh = o[:, 256 + h * HD:256 + (h + 1) * HD]
                            mm(oh, rp0[:, h, P:T], rv[:, 0, h, :], True, False)
                            last = mm(oh, rp1[:, h, :], rv[:, 1, h, :], False, True)
                        is_full(last, l, stage)
                    elif stage == "convT":
                        o = begin(l, stage)
                        pe.wait_ge(s_conv, l + 1)
                        for i in range(NT):
                            for c in range(NC):
                                q = i * NC + c
                                last = flip(o[:, q * P:(q + 1) * P], cacc[:, 0, c, i * P:(i + 1) * P])
                        is_full(last, l, stage)
                    elif stage == "convB":
                        o = begin(l, stage)
                        pe.wait_ge(s_cln, l + 1)
                        for c in range(NC):
                            for i in range(NT):
                                q = c * NT + i
                                last = flip(o[:, q * P:(q + 1) * P], cln[:, i, c * P:(c + 1) * P])
                        is_full(last, l, stage)
                    elif stage == "conv_pw":
                        o = begin(l, stage)
                        freed(pe, l, "convB")
                        w = item(5)[:, 16 * CMP_HID + 2 * HD:].rearrange("p (c n) -> p c n", c=NC)
                        for m in range(NC):
                            for c in range(NC):
                                last = mm(o[:, m * T:(m + 1) * T], w[:, c, m * P:(m + 1) * P], cact[:, c, :],
                                          c == 0, c == NC - 1)
                        is_full(last, l, stage)
                    elif stage == "attn_sum":
                        o = begin(l, stage, k)
                        pe.wait_ge(s_osum, l * NT + k + 1)
                        for q in range(4):
                            last = flip(o[:, q * P:(q + 1) * P],
                                        obr[:, 0, k, 2 * q:2 * q + 2, :].rearrange("p h d -> p (h d)"))
                        is_full(last, l, stage, k)
                    elif stage == "retcat":
                        o = begin(l, stage)
                        pe.wait_ge(s_ret, l + 1)
                        for m in range(2):
                            for i in range(NT):
                                q = m * NT + i
                                last = flip(o[:, q * P:(q + 1) * P],
                                            ro[:, i, 2 * m:2 * m + 2, :].rearrange("p h d -> p (h d)"))
                        is_full(last, l, stage)
                    elif stage == "out":
                        w = item(6 + k).rearrange("p (k n) -> p k n", k=KD)
                        if k == 0:
                            for i in range(NT):
                                freed(pe, l, "attn_sum", i)
                        landed(l, 6 + k)
                        for i in range(NT):
                            o = begin(l, stage, k, i)
                            for c in range(KD // 2):
                                mm(o, catT[:, c, i * P:(i + 1) * P], w[:, c, :], c == 0, False)
                    elif stage == "out_rest":
                        w = item(6 + k).rearrange("p (k n) -> p k n", k=KD)
                        if k == 0:
                            freed(pe, l, "retcat")
                            freed(pe, l, "conv_pw")
                        for i in range(NT):
                            for c in range(KD // 2, KD):
                                last = mm(bank(l, "out", k, i), catT[:, c, i * P:(i + 1) * P], w[:, c, :], False,
                                          c == KD - 1)
                            is_full(last, l, "out", k, i)

            def three(o, ah, al, bh, bl, first, final):
                mm(o, ah, bh, first, False)
                mm(o, ah, bl, False, False)
                return mm(o, al, bh, False, final)

            def up(tiles, p, r):
                for i in range(tiles):
                    for h in range(2):
                        k = 2 * p + h
                        w = slice(h * 512, (h + 1) * 512)
                        last = three(ps[:, i, :], hTh[:, k, i * P:(i + 1) * P], hTl[:, k, i * P:(i + 1) * P],
                                     wh[:, r, w], wl[:, r, w], k == 0, k == KD - 1)
                last.then_inc(s_piece, 1)

            def turn(tiles, u):
                for i in range(tiles):
                    pe.wait_ge(s_gated, u + i + 1)
                    for c in range(FC // P):
                        last = flip(ps[:, 2 + i, c * P:(c + 1) * P], gated[:, i, c * P:(c + 1) * P])
                    last.then_inc(s_gtp, 1)

            def down(tiles, q, c, r, first, final):
                pe.wait_ge(s_lo, q + 1)
                for i in range(tiles):
                    for n in range(2):
                        w = slice(n * 512, (n + 1) * 512)
                        last = three(ps[:, 4 + 2 * i + n, :], gTh[:, i, c, :], gTl[:, i, c, :], wh[:, r, w],
                                     wl[:, r, w], first and c == 0, final and c == DOWN - 1)
                last.then_inc(s_piece, 1)

            def step(tiles, u0, q0, j, g=0, before_sums=None):
                u = u0 + j * tiles + g * (SLOTS * tiles)
                q = q0 + g * (SLOTS * PIECES)
                for p in range(UP):
                    at = up_at(j, p)
                    if p == 0 and not (isinstance(u, int) and u == 0):
                        pe.wait_ge(s_gated, u)
                        if j:
                            turn(tiles, u - tiles)
                    pe.wait_ge(s_lo, q + (at + 1))
                    up(tiles, p, at % PIECES)
                if before_sums is not None:
                    before_sums()
                if j:
                    pe.wait_ge(s_gTl, u)
                    for c in range(DOWN):
                        at = up_at(j, UP) + c
                        down(tiles, q + at, c, at % PIECES, j == 1, False)

            def steps(tiles, u0, q0, before_sums=None):
                step(tiles, u0, q0, 1, before_sums=before_sums)
                with pe.Fori(0, (STEPS - 2) // SLOTS) as g:
                    for j in range(2, 2 + SLOTS):
                        step(tiles, u0, q0, j, g)
                turn(tiles, u0 + tiles * (STEPS - 1))

            def last_down(tiles, u0, q0):
                pe.wait_ge(s_gTl, u0 + tiles * STEPS)
                for c in range(DOWN):
                    at = down_at(STEPS - 1, c)
                    down(tiles, q0 + at, c, at % PIECES, False, True)

            def dense():
                pe.wait_ge(s_hTl, 4)
                step(NT, 0, 0, 0)
                steps(NT, 0, 0)
                last_down(NT, 0, 0)

            def gather(n):
                pe.wait_ge(s_pick, n + 1)
                for half in range(2):
                    for q in range(4):
                        c = 4 * half + q
                        for i in range(NT):
                            for part in range(3):
                                last = mm(ps[:, 6 + half, q * P:(q + 1) * P], xb[part][:, i, c * P:(c + 1) * P],
                                          pick[:, i, :], i == part == 0, i == NT - 1 and part == 2)
                    last.then_inc(s_gather, 1)

            def expert(e, rnd, follows):
                ex = e + rnd * EXPERTS
                ue = NT * STEPS + ex * STEPS
                qe = PASS + ex * PASS

                def pick_turned():
                    pe.wait_ge(s_xadd, 4 * ex + 1)
                    for i in range(NT):
                        last = mm(ps[:, 3, i * P:(i + 1) * P], pick[:, i, :], identb[:], True, True)
                    last.then_inc(s_spt, 1)

                steps(1, ue, qe, pick_turned)
                if follows:
                    gather(ex + 1)
                last_down(1, ue, qe)
                if follows:
                    pe.wait_ge(s_xel, 2 * ex + 4)
                    step(1, ue + STEPS, qe + PASS, 0)
                pe.wait_ge(s_sptc, ex + 1)
                for n in range(2):
                    pe.wait_ge(s_yel, 2 * ex + (n + 1))
                    for i in range(NT):
                        mm(ps[:, SCATTER[i][n], :], pickT[:, i, :], yeh[:, n, :], True, False)
                        mm(ps[:, SCATTER[i][n], :], pickT[:, i, :], yel[:, n, :], False, True).then_inc(s_scat, 1)

            def experts(rnd):
                if rnd:
                    pe.wait_ge(s_xadd, 4 * EXPERTS + 1)
                else:
                    pe.wait_ge(s_xb2, NT)
                gather(rnd * EXPERTS)
                pe.wait_ge(s_xel, 2 * rnd * EXPERTS + 2)
                first = rnd * EXPERTS
                step(1, NT * STEPS + first * STEPS, PASS + first * PASS, 0)
                with pe.Fori(0, EXPERTS - 1) as e:
                    expert(e, rnd, True)
                expert(EXPERTS - 1, rnd, False)

            pe.wait_ge(s_in, INPUTS * 16)
            mixer(0)
            dense()
            mixer(1)
            pe.wait_ge(s_late, 32)
            for q in range(4):
                freed(pe, 1, "norm", 1, q)
            for i in range(NT):
                for k in range(KD):
                    last = mm(ps[:, 0, i * EXPERTS:(i + 1) * EXPERTS], hT[:, k, i * P:(i + 1) * P], router[:, k, :],
                              k == 0, k == KD - 1)
            last.then_inc(s_logit, 1)
            pe.wait_ge(s_sel, 1)
            n = EXPERTS
            mm(ps[:, 1, 0:n], const("before"), sel[:, 0, :], True, True)
            mm(ps[:, 1, n:2 * n], const("before"), sel[:, 1, :], True, False)
            mm(ps[:, 1, n:2 * n], const("ones"), sel[:, 0, :], False, True)
            mm(ps[:, 1, 2 * n:3 * n], const("ones"), sel[:, 0, :], True, False)
            mm(ps[:, 1, 2 * n:3 * n], const("ones"), sel[:, 1, :], False, True).then_inc(s_rankp, 1)
            pe.wait_ge(s_over, 1)
            experts(0)
            more = pe.value_load(over[0:1, 0:1], min_val=0, max_val=1)
            with pe.If(more > 0):
                experts(1)

        @block.scalar
        def _(act):
            A = nc.scalar.activation

            def rms_squares(n):
                for i in range(NT):
                    A(xn[:, i, :], x[:, i, :], ACT.Square, accum_out=stat[:, 0, i:i + 1]).then_inc(s_ss, 1)
                act.wait_ge(s_ms, n + 1)
                A(stat[:, 2, :], stat[:, 1, :], ACT.Sqrt).then_inc(s_root, 1)

            def mixer(l):
                for stage, k in MIXER:
                    if stage == "norm":
                        if k == 0 and l == 0:
                            act.wait_ge(s_x, 16)
                        elif k == 0:
                            act.wait_ge(s_dense, 4)
                        else:
                            for q in range(4):
                                freed(act, l, "out", q // 2, q % 2)
                        rms_squares(2 * l + k)
                        if k == 0 and l == 0:
                            act.wait_ge(s_in, INPUTS * 16)
                    elif stage == "q":
                        full(act, l, stage, k)
                        is_free(A(qT[:, 2 * k:2 * k + 2, :], bank(l, stage, k).rearrange("p (c t) -> p c t", c=2),
                                  ACT.Copy), l, stage, k)
                    elif stage == "cg":
                        full(act, l, stage)
                        is_free(A(sig[:], bank(l, stage).rearrange("p (c t) -> p c t", c=NC), ACT.Sigmoid), l, stage)
                    elif stage == "vsw":
                        full(act, l, stage)
                        is_free(A(vv[:].rearrange("p i b g d -> p (i b g d)"), bank(l, stage), ACT.Copy), l, stage)
                    elif stage == "rvg":
                        full(act, l, stage, k)
                        o = bank(l, stage, k)
                        A(rv[:, k, :, :].rearrange("p h d -> p (h d)"), o[:, 0:256], ACT.Copy)
                        is_free(A(rgate[:, k, :, :].rearrange("p h d -> p (h d)"), o[:, 256:512], ACT.Silu),
                                l, stage, k)
                    elif stage == "gl":
                        full(act, l, stage)
                        is_free(A(gates[:].rearrange("p i h b -> p (i h b)"), bank(l, stage)[:, 0:NT * 24],
                                  ACT.Sigmoid), l, stage)
                    elif stage == "score":
                        br, g, i, c0, n = UNITS[k]
                        keys = (i + 1) * P
                        act.wait_ge(s_amax, l * len(UNITS) + k + 1)
                        if k >= 3:
                            full(act, l, "probT", k - 3)
                        for c in range(n):
                            last = A(prob[:, k % 3, c * keys:(c + 1) * keys],
                                     bank(l, stage, k)[:, c * keys:(c + 1) * keys], ACT.Exp,
                                     bias=nmax[:, k, c:c + 1], scale=SCALE, accum_out=asum[:, k, c:c + 1])
                        last.then_inc(s_exp, 1)
                        act.wait_ge(s_exp, l * len(UNITS) + k + 1)
                        is_free(act.nop(), l, stage, k)
                    elif stage == "probT":
                        if k >= 3:
                            full(act, l, "pv", k - 3)
                        full(act, l, stage, k)
                        is_free(A(probT[:, k % 3, :], bank(l, stage, k), ACT.Copy), l, stage, k)
                    elif stage == "hid":
                        full(act, l, stage, k)
                        is_free(A(hrow[:, k, :], bank(l, stage, k)[0:2 * CB, 0:CMP_HID], ACT.Silu), l, stage, k)
                    elif stage == "hidT":
                        full(act, l, stage, k)
                        o = bank(l, stage, k)[:, 0:64]
                        if k == 0:
                            ins = A(hid[:, 0, :, :].rearrange("p m n -> p (m n)"), o, ACT.Copy)
                        else:
                            ins = A(hidv[:], spread(o.rearrange("p (q c) -> p q c", q=4), 2, HPG), ACT.Copy)
                        is_free(ins, l, stage, k)
                    elif stage == "cscore":
                        act.wait_ge(s_cs2, l + 1)
                        A(cs[:], cs2[:], ACT.Exp).then_inc(s_cexp, 1)
                    elif stage == "cprobT":
                        full(act, l, stage)
                        is_free(A(cprobT[:], bank(l, stage)[:, 0:T].rearrange("p (i q) -> p i q", i=NT), ACT.Copy),
                                l, stage)
                    elif stage == "cpv":
                        full(act, l, stage, k)
                        is_free(A(obr[:, 2, k, :, :].rearrange("p h d -> p (h d)"), bank(l, stage, k), ACT.Copy),
                                l, stage, k)
                    elif stage == "retT":
                        full(act, l, stage, k)
                        is_free(A(rT[:, :, k * P:(k + 1) * P], bank(l, stage, k).rearrange("p (q t) -> p q t", q=4),
                                  ACT.Copy), l, stage, k)
                    elif stage == "convT":
                        act.wait_ge(s_cvar, l + 1)
                        A(clst[:, 3, :], clst[:, 2, :], ACT.Sqrt).then_inc(s_croot, 1)
                    elif stage == "retnorm":
                        act.wait_ge(s_rvar, l + 1)
                        A(rst[:, 3, :, :], rst[:, 2, :, :], ACT.Sqrt).then_inc(s_rroot, 1)
                    elif stage == "convB":
                        full(act, l, stage)
                        g, b = param(l, "conv_g"), param(l, "conv_beta")
                        for c in range(NC):
                            last = A(cact[:, c, :], bank(l, stage)[:, c * T:(c + 1) * T], ACT.Silu,
                                     bias=b[:, c:c + 1], scale=g[:, c:c + 1])
                        is_free(last, l, stage)
                    elif stage == "attn_sum":
                        full(act, l, stage, k)
                        is_free(A(catT[:, 0:4, k * P:(k + 1) * P],
                                  bank(l, stage, k).rearrange("p (q t) -> p q t", q=4), ACT.Copy), l, stage, k)
                    elif stage in ("conv_pw", "retcat"):
                        full(act, l, stage)
                        m = 4 if stage == "conv_pw" else 6
                        is_free(A(catT[:, m:m + 2, :], bank(l, stage).rearrange("p (q t) -> p q t", q=2), ACT.Copy),
                                l, stage)

            def hi(q, r, raw):
                if not isinstance(q, int) or q >= PIECES:
                    act.wait_ge(s_piece, q - (PIECES - 1))
                A(wh[:, r, :], raw, ACT.Copy).then_inc(s_hi, 1)

            def ups(q0, up0, j, parts, g=0):
                s = j % SLOTS
                if 0 in parts:
                    act.wait_ge(slot_full[s], 16 * (up0[s] + (j // SLOTS + 1) + g))
                for p in parts:
                    hi(q0 + up_at(j, p) + g * (SLOTS * PIECES), up_at(j, p) % PIECES,
                       ring[:, s, p * PIECE:(p + 1) * PIECE])

            def turned(tiles, u0, j, g=0):
                for i in range(tiles):
                    act.wait_ge(s_gtp, u0 + (j * tiles + i + 1) + g * (SLOTS * tiles))
                    A(gTh[:, i, :, :], ps[:, 2 + i, 0:FC].rearrange("p (c t) -> p c t", c=DOWN), ACT.Copy)\
                        .then_inc(s_gTh, 1)

            def steps(tiles, u0, q0, up0, down0, before_last=None):
                def downs(j, g):
                    s = j % SLOTS
                    act.wait_ge(down_full[s], 16 * (down0[s] + (j // SLOTS + 1) + g))
                    for c in range(DOWN):
                        hi(q0 + down_at(j, c) + g * (SLOTS * PIECES), down_at(j, c) % PIECES,
                           ring[:, s, (UP + c) * PIECE:(UP + c + 1) * PIECE])

                def hidden(j, g):
                    for i in range(tiles):
                        act.wait_ge(s_piece, q0 + (up_at(j, UP - 1) + 1) + g * (SLOTS * PIECES))
                        A(silu[:, i, :], ps[:, i, 0:FC], ACT.Silu).then_inc(s_silu, 1)

                def step(j, g):
                    hidden(j - 1, g)
                    ups(q0, up0, j, range(UP // 2, UP), g)
                    turned(tiles, u0, j - 1, g)
                    downs(j - 1, g)

                with act.Fori(0, (STEPS - 2) // SLOTS) as g:
                    for j in range(1, 1 + SLOTS):
                        step(j, g)
                        ups(q0, up0, j + 1, range(UP // 2), g)
                if before_last is not None:
                    before_last()
                step(STEPS - 1, 0)
                hidden(STEPS - 1, 0)
                downs(STEPS - 1, 0)

            def dense():
                ups(0, MIX_FILLS, 0, range(UP))
                for q in range(4):
                    i, half = divmod(q, 2)
                    freed(act, 0, "norm", 1, q)
                    z = (slice(None), slice(4 * half, 4 * half + 4), slice(i * P, (i + 1) * P))
                    A(hTh[z], hT[z], ACT.Copy).then_inc(s_hTh, 1)
                ups(0, MIX_FILLS, 1, range(UP // 2))
                steps(NT, 0, 0, MIX_FILLS, [0] * SLOTS)
                turned(NT, 0, STEPS - 1)

            def fills(ex):
                return ([mix_fill(1, LAST_ITEM[s]) + FFN_FILLS[s] * ex for s in range(SLOTS)],
                        [FFN_FILLS[s] * (ex + 1) for s in range(SLOTS)])

            def picked(n):
                for half in range(2):
                    act.wait_ge(s_gather, 2 * n + (half + 1))
                    for q in range(4):
                        c = 4 * half + q
                        last = A(hTh[:, c, 0:P], ps[:, 6 + half, q * P:(q + 1) * P], ACT.Copy,
                                 scale=param(1, "ln_ffn")[:, c:c + 1])
                    last.then_inc(s_xeh, 1)

            def expert(e, rnd, follows):
                ex = e + rnd * EXPERTS
                ue = NT * STEPS + ex * STEPS
                qe = PASS + ex * PASS

                def pick_turned():
                    act.wait_ge(s_spt, ex + 1)
                    A(pickT, ps[:, 3, 0:T].rearrange("p (i t) -> p i t", i=NT), ACT.Copy).then_inc(s_sptc, 1)

                steps(1, ue, qe, *fills(ex), pick_turned)
                turned(1, ue, STEPS - 1)
                if follows:
                    ups(qe + PASS, fills(ex + 1)[0], 0, range(UP // 2))
                    picked(ex + 1)
                    ups(qe + PASS, fills(ex + 1)[0], 0, range(UP // 2, UP))
                act.wait_ge(s_piece, qe + PASS)
                for n in range(2):
                    A(yeh[:, n, :], ps[:, 4 + n, :], ACT.Copy).then_inc(s_yeh, 1)
                if follows:
                    ups(qe + PASS, fills(ex + 1)[0], 1, range(UP // 2))

            def experts(rnd):
                first = rnd * EXPERTS
                q0 = PASS + first * PASS
                if rnd:
                    ups(q0, fills(first)[0], 0, range(UP))
                picked(first)
                ups(q0, fills(first)[0], 1, range(UP // 2))
                with act.Fori(0, EXPERTS - 1) as e:
                    expert(e, rnd, True)
                expert(EXPERTS - 1, rnd, False)

            mixer(0)
            dense()
            mixer(1)
            ups(PASS, fills(0)[0], 0, range(UP))
            act.wait_ge(s_logit, 1)
            for i in range(NT):
                A(xb[0][:, i, :], xn[:, i, :], ACT.Copy).then_inc(s_xb, 1)
            act.wait_ge(s_m1, 2)
            A(rwork[:, 1, :, :], rwork[:, 0, :, :], ACT.Exp).then_inc(s_rexp, 1)
            for i in range(NT):
                act.wait_ge(s_xr, i + 1)
                A(xb[1][:, i, :], xn[:, i, :], ACT.Copy).then_inc(s_xb, 1)
            act.wait_ge(s_over, 1)
            experts(0)
            more = act.value_load(over[0:1, 0:1], min_val=0, max_val=1)
            with act.If(more > 0):
                experts(1)
            act.wait_ge(s_last, 1)
            rms_squares(2 * DEPTH)

        @block.vector
        def _(dve):
            V = nc.vector
            made = [0]

            def link(ins):
                made[0] += 1
                ins.then_inc(v_done, 1)
                dve.wait_ge(v_done, made[0])

            def rms_apply(n, gain=None):
                dve.wait_ge(s_ss, NT * (n + 1))
                V.tensor_scalar(stat[:, 1, :], stat[:, 0, :], 1.0 / D, EPS, ALU.mult, ALU.add).then_inc(s_ms, 1)
                dve.wait_ge(s_root, n + 1)
                link(V.reciprocal(stat[:, 3, :], stat[:, 2, :]))
                if gain is None:
                    for i in range(NT):
                        V.tensor_scalar(xn[:, i, :], x[:, i, :], stat[:, 3, i:i + 1], None, ALU.mult)\
                            .then_inc(s_xn, 1)
                else:
                    for i in range(NT):
                        V.scalar_tensor_tensor(out=res[:, i, :], in0=x[:, i, :], scalar=stat[:, 3, i:i + 1],
                                               in1=gain, op0=ALU.mult, op1=ALU.mult).then_inc(s_res, 1)

            def conv_part(l, part):
                w = param(l, "conv_w").rearrange("p (c k) -> p c k", c=NC)
                b = param(l, "conv_b")
                taps = range(part * CONV_K // CONV_PARTS, (part + 1) * CONV_K // CONV_PARTS)
                for k in taps:
                    for c in range(NC):
                        win = hc[:, c, k:k + T]
                        o = cacc[:, (CONV_K - 1 - k) % 2, c, :]
                        if k == 0:
                            ins = V.tensor_scalar(o, win, w[:, c, 0:1], b[:, c:c + 1], ALU.mult, ALU.add)
                        else:
                            ins = V.scalar_tensor_tensor(out=o, in0=win, scalar=w[:, c, k:k + 1],
                                                         in1=cacc[:, (CONV_K - k) % 2, c, :], op0=ALU.mult,
                                                         op1=ALU.add)
                    if k == CONV_K - 1:
                        ins.then_inc(s_conv, 1)
                    else:
                        link(ins)

            def mixer(l):
                for g in range(2):
                    last = V.memset(kT[(1 - g) * HD:(2 - g) * HD, g, :, :], 0.0)
                last.then_inc(s_zero, 1)
                for stage, k in MIXER:
                    if stage == "norm":
                        rms_apply(2 * l + k)
                        if k == 0 and l == 0:
                            dve.wait_ge(s_in, INPUTS * 16)
                            V.tensor_copy(identb[:], ident)
                            V.tensor_copy(causalb[:], const("causal")).then_inc(s_zero, 1)
                        gain = param(l, "ln_attn" if k == 0 else "ln_ffn")
                        for q in range(4):
                            i, half = divmod(q, 2)
                            full(dve, l, stage, k, q)
                            is_free(V.tensor_tensor(hT[:, 4 * half:4 * half + 4, i * P:(i + 1) * P],
                                                    bank(l, stage, k, q).rearrange("p (c t) -> p c t", c=4),
                                                    spread(gain[:, 4 * half:4 * half + 4], 2, P), ALU.mult),
                                    l, stage, k, q)
                    elif stage == "ks":
                        full(dve, l, stage)
                        for g in range(2):
                            z = slice(g * HD, (g + 1) * HD)
                            last = V.tensor_copy(kT[z, g, :, :],
                                                 bank(l, stage)[z, :].rearrange("p (c t) -> p c t", c=2))
                        is_free(last, l, stage)
                    elif stage == "kcv":
                        full(dve, l, stage)
                        src = bank(l, stage).rearrange("p (v c j r) -> p v j c r", v=2, c=CB, j=8, r=2)
                        pe_ = param(l, "pe").rearrange("p (v h j) -> p v h j", v=2, h=2)
                        for g in range(2):
                            for r in range(2):
                                for hi in range(2):
                                    lo = r * HD
                                    for v in range(2):
                                        last = V.tensor_tensor(
                                            blocks[lo:lo + HD, v, hi, :, g, 0:NBLK],
                                            src[g * HD:(g + 1) * HD, v, :, hi:hi + NBLK, r],
                                            spread(pe_[lo:lo + HD, v, hi, :], 2, NBLK), ALU.add)
                        is_free(last, l, stage)
                    elif stage == "ca":
                        full(dve, l, stage)
                        freed(dve, l, "cg")
                        is_free(V.tensor_tensor(hc[:, :, CONV_K - 1:], bank(l, stage).rearrange("p (c t) -> p c t", c=NC),
                                                sig[:], ALU.mult), l, stage)
                        freed(dve, l, "ca")
                    elif stage == "conv":
                        conv_part(l, k)
                    elif stage == "score":
                        br, g, i, c0, n = UNITS[k]
                        full(dve, l, stage, k)
                        keys = (i + 1) * P
                        link(V.tensor_reduce(amax[:, k, 0:n], bank(l, stage, k).rearrange("p (n k) -> p n k", n=n),
                                             AX.X, ALU.max))
                        V.tensor_scalar(nmax[:, k, 0:n], amax[:, k, 0:n], -SCALE, None, ALU.mult)\
                            .then_inc(s_amax, 1)
                    elif stage == "pv":
                        br, g, i, c0, n = UNITS[k]
                        dve.wait_ge(s_exp, l * len(UNITS) + k + 1)
                        link(V.reciprocal(arec[:, k, 0:n], asum[:, k, 0:n]))
                        if k == 0:
                            freed(dve, l, "gl")
                        h0 = g * HPG + c0
                        link(V.tensor_tensor(awgt[:, k, 0:n], arec[:, k, 0:n], gates[:, i, h0:h0 + n, 1 + br],
                                             ALU.mult))
                        full(dve, l, stage, k)
                        is_free(V.tensor_tensor(obr[:, br, i, h0:h0 + n, :],
                                                bank(l, stage, k)[:, 0:n * HD].rearrange("p (n d) -> p n d", n=n),
                                                spread(awgt[:, k, 0:n], 2, HD), ALU.mult), l, stage, k)
                    elif stage == "rqk":
                        full(dve, l, stage, k)
                        if l == 0 and k == 0:
                            dve.wait_ge(s_const, 16)
                        o = bank(l, stage, k).rearrange("p (h s d) -> p h s d", h=8, s=2)
                        oh = bank(l, stage, k).rearrange("p (h d) -> p h d", h=8)
                        cos = const("cos").rearrange("p (i d) -> p i d", i=NT)[:, k, :]
                        sin = const("sin").rearrange("p (i s d) -> p i s d", i=NT, s=2)[:, k, :, :]
                        V.tensor_tensor(rot[:, 0, :, :], oh, spread(cos, 1, 8), ALU.mult)
                        r1 = rot[:, 1, :, :].rearrange("p h (s d) -> p h s d", s=2)
                        V.tensor_tensor(r1[:, :, 0, :], o[:, :, 1, :], spread(sin[:, 0, :], 1, 8), ALU.mult)
                        link(V.tensor_tensor(r1[:, :, 1, :], o[:, :, 0, :], spread(sin[:, 1, :], 1, 8), ALU.mult))
                        is_free(V.tensor_tensor(rqk[:, k, :, :], rot[:, 0, :, :], rot[:, 1, :, :], ALU.add),
                                l, stage, k)
                        freed(dve, l, stage, k)
                    elif stage == "cmpkv":
                        full(dve, l, stage)
                        o = bank(l, stage)
                        V.tensor_copy(kc[:], o[:, 0:2 * CB])
                        is_free(V.tensor_tensor(vblk[:], spread(o[:, HD:2 * HD], 1, HEADS),
                                                spread(const("head_block"), 2, HD), ALU.mult), l, stage)
                    elif stage == "cscore":
                        add = const("cmp_add").rearrange("p (i c) -> p i c", i=NT)
                        keep = const("cmp_keep").rearrange("p (i c) -> p i c", i=NT)
                        for g in range(2):
                            full(dve, l, stage, 0, g)
                            o = bank(l, stage, 0, g)[:, 0:NT * HPG * CB].rearrange("p (i h c) -> p i h c", i=NT, h=HPG)
                            for i in range(NT):
                                last = V.scalar_tensor_tensor(out=cs[:, i, g * HPG:(g + 1) * HPG, :], in0=o[:, i, :, :],
                                                              scalar=SCALE, in1=spread(add[:, i, :], 1, HPG),
                                                              op0=ALU.mult, op1=ALU.add)
                            is_free(last, l, stage, 0, g)
                        freed(dve, l, stage, 0, 1)
                        c3 = cs[:].rearrange("p i h c -> p (i h) c")
                        st = cstat[:].rearrange("p s i h -> p s (i h)")
                        link(V.tensor_reduce(st[:, 0, :], c3, AX.X, ALU.max))
                        V.tensor_tensor(cs2[:].rearrange("p i h c -> p (i h) c"), c3, spread(st[:, 0, :], 2, CB),
                                        ALU.subtract).then_inc(s_cs2, 1)
                        dve.wait_ge(s_cexp, l + 1)
                        link(V.tensor_reduce(st[:, 1, :], c3, AX.X, ALU.add))
                        link(V.reciprocal(st[:, 2, :], st[:, 1, :]))
                        V.tensor_tensor(cstat[:, 3, :, :], cstat[:, 2, :, :], gates[:, :, :, 0], ALU.mult)
                        for i in range(NT):
                            last = V.tensor_tensor(cs2[:, i, :, :], cs[:, i, :, :], spread(keep[:, i, :], 1, HEADS),
                                                   ALU.mult)
                        link(last)
                        V.tensor_tensor(cprob[:].rearrange("p i h c -> p (i h) c"),
                                        cs2[:].rearrange("p i h c -> p (i h) c"), spread(st[:, 3, :], 2, CB),
                                        ALU.mult).then_inc(s_cprob, 1)
                    elif stage == "rets":
                        b, t = k % 2, k // 2
                        full(dve, l, stage, k)
                        n = T - t * P
                        dec = const("decay").rearrange("p (u b t) -> p u b t", u=2, b=2)[:, :, b, 0:n]
                        dst = (rp0 if t == 0 else rp1)[:].rearrange("p (u b) t -> p u b t", b=2)[:, :, b, :]
                        is_free(V.tensor_tensor(dst, bank(l, stage, k)[:, 0:2 * n].rearrange("p (u t) -> p u t", u=2),
                                                dec, ALU.mult), l, stage, k)
                    elif stage == "reto":
                        full(dve, l, stage)
                        o = bank(l, stage).rearrange("p (i h d) -> p i h d", i=NT, h=RET_HEADS)
                        is_free(V.tensor_copy(ro[:], o), l, stage)
                        freed(dve, l, stage)
                    elif stage == "retnorm":
                        r3 = ro[:].rearrange("p i h d -> p (i h) d")
                        q3 = rsq.rearrange("p i h d -> p (i h) d")
                        st = rst[:].rearrange("p s i h -> p s (i h)")
                        link(V.tensor_reduce(st[:, 0, :], r3, AX.X, ALU.add))
                        link(V.tensor_scalar(st[:, 1, :], st[:, 0, :], 1.0 / HD, None, ALU.mult))
                        link(V.tensor_tensor(r3, r3, spread(st[:, 1, :], 2, HD), ALU.subtract))
                        link(V.tensor_tensor(q3, r3, r3, ALU.mult))
                        link(V.tensor_reduce(st[:, 0, :], q3, AX.X, ALU.add))
                        V.tensor_scalar(st[:, 2, :], st[:, 0, :], 1.0 / HD, LN_EPS, ALU.mult, ALU.add)\
                            .then_inc(s_rvar, 1)
                        gn = param(l, "ret_gn").rearrange("p (h d) -> p h d", h=RET_HEADS)
                        freed(dve, l, "rvg", 0)
                        freed(dve, l, "rvg", 1)
                        for i in range(NT):
                            last = V.tensor_tensor(rsq[:, i, :, :], rgate[:, i, :, :], gn, ALU.mult)
                        dve.wait_ge(s_rroot, l + 1)
                        link(V.reciprocal(st[:, 4, :], st[:, 3, :]))
                        link(V.tensor_tensor(r3, r3, spread(st[:, 4, :], 2, HD), ALU.mult))
                        V.tensor_tensor(r3, r3, q3, ALU.mult).then_inc(s_ret, 1)
                    elif stage == "convT":
                        full(dve, l, stage)
                        link(V.tensor_reduce(clst[:, 0, :], bank(l, stage).rearrange("p (i c) -> p i c", i=NT), AX.X,
                                             ALU.add))
                        link(V.tensor_scalar(clst[:, 1, :], clst[:, 0, :], 1.0 / CONV_CH, None, ALU.mult))
                        is_free(V.tensor_tensor(cln[:], bank(l, stage).rearrange("p (i c) -> p i c", i=NT),
                                                spread(clst[:, 1, :], 2, CONV_CH), ALU.subtract), l, stage)
                        freed(dve, l, stage)
                        link(V.tensor_tensor(csq[:], cln[:], cln[:], ALU.mult))
                        link(V.tensor_reduce(clst[:, 0, :], csq[:], AX.X, ALU.add))
                        V.tensor_scalar(clst[:, 2, :], clst[:, 0, :], 1.0 / CONV_CH, LN_EPS, ALU.mult, ALU.add)\
                            .then_inc(s_cvar, 1)
                        dve.wait_ge(s_croot, l + 1)
                        link(V.reciprocal(clst[:, 4, :], clst[:, 3, :]))
                        V.tensor_tensor(cln[:], cln[:], spread(clst[:, 4, :], 2, CONV_CH), ALU.mult)\
                            .then_inc(s_cln, 1)
                    elif stage == "attn_sum":
                        freed(dve, l, "cpv", k)
                        for u in (1, 2, 4, 5, 7, 8, 10, 11) if k else (0, 3, 6, 9):
                            freed(dve, l, "pv", u)
                        link(V.tensor_tensor(obr[:, 1, k, :, :], obr[:, 1, k, :, :], obr[:, 2, k, :, :], ALU.add))
                        V.tensor_tensor(obr[:, 0, k, :, :], obr[:, 0, k, :, :], obr[:, 1, k, :, :], ALU.add)\
                            .then_inc(s_osum, 1)
                    elif stage == "out_rest":
                        for i in range(NT):
                            full(dve, l, "out", k, i)
                            xs = x[:, i, k * 512:(k + 1) * 512]
                            is_free(V.tensor_tensor(xs, bank(l, "out", k, i), xs, ALU.add), l, "out", k, i)

            def lo(q, r, raw):
                dve.wait_ge(s_hi, q + 1)
                V.tensor_tensor(wl[:, r, :], raw, wh[:, r, :].bitcast(F32), ALU.subtract).then_inc(s_lo, 1)

            def ups(q0, j, parts, g=0):
                for p in parts:
                    lo(q0 + up_at(j, p) + g * (SLOTS * PIECES), up_at(j, p) % PIECES,
                       ring[:, j % SLOTS, p * PIECE:(p + 1) * PIECE])

            def turned(tiles, u0, j, g=0):
                for i in range(tiles):
                    dve.wait_ge(s_gTh, u0 + (j * tiles + i + 1) + g * (SLOTS * tiles))
                    V.tensor_tensor(gTl[:, i, :, :], ps[:, 2 + i, 0:FC].rearrange("p (c t) -> p c t", c=DOWN),
                                    gTh[:, i, :, :].bitcast(F32), ALU.subtract).then_inc(s_gTl, 1)

            def steps(tiles, u0, q0, before_last=None):
                def downs(j, g):
                    for c in range(DOWN):
                        lo(q0 + down_at(j, c) + g * (SLOTS * PIECES), down_at(j, c) % PIECES,
                           ring[:, j % SLOTS, (UP + c) * PIECE:(UP + c + 1) * PIECE])

                def hidden(j, g):
                    for i in range(tiles):
                        dve.wait_ge(s_silu, u0 + (j * tiles + i + 1) + g * (SLOTS * tiles))
                        V.tensor_tensor(gated[:, i, :], ps[:, i, FC:2 * FC], silu[:, i, :], ALU.mult)\
                            .then_inc(s_gated, 1)

                def step(j, g):
                    hidden(j - 1, g)
                    ups(q0, j, range(UP // 2, UP), g)
                    turned(tiles, u0, j - 1, g)
                    downs(j - 1, g)

                with dve.Fori(0, (STEPS - 2) // SLOTS) as g:
                    for j in range(1, 1 + SLOTS):
                        step(j, g)
                        ups(q0, j + 1, range(UP // 2), g)
                if before_last is not None:
                    before_last()
                step(STEPS - 1, 0)
                hidden(STEPS - 1, 0)
                downs(STEPS - 1, 0)

            def dense():
                for q in range(4):
                    i, half = divmod(q, 2)
                    dve.wait_ge(s_hTh, q + 1)
                    z = (slice(None), slice(4 * half, 4 * half + 4), slice(i * P, (i + 1) * P))
                    V.tensor_tensor(hTl[z], hT[z], hTh[z].bitcast(F32), ALU.subtract).then_inc(s_hTl, 1)
                ups(0, 0, range(UP))
                ups(0, 1, range(UP // 2))
                steps(NT, 0, 0)
                turned(NT, 0, STEPS - 1)
                dve.wait_ge(s_piece, PASS)
                for i in range(NT):
                    for n in range(2):
                        xs = x[:, i, n * 512:(n + 1) * 512]
                        V.tensor_tensor(xs, ps[:, 4 + 2 * i + n, :], xs, ALU.add).then_inc(s_dense, 1)

            def routing():
                ups(PASS, 0, range(UP))
                dve.wait_ge(s_logit, 1)
                lg = logit
                V.memset(sel[:], 0.0)
                V.memset(gate[:], 0.0)
                link(V.tensor_copy(lg[:], ps[:, 0, 0:NT * EXPERTS].rearrange("p (i e) -> p i e", i=NT)))
                tie = const("earlier").rearrange("p (e f) -> p e f", e=EXPERTS)
                for i in range(NT):
                    mine, other = spread(lg[:, i, :], 2, EXPERTS), spread(lg[:, i, :], 1, EXPERTS)
                    V.tensor_tensor(rcmp[:, 0, i, :, :], other, mine, ALU.is_gt)
                    link(V.tensor_tensor(rcmp[:, 1, i, :, :], other, mine, ALU.is_equal))
                    link(V.tensor_tensor(rcmp[:, 2, i, :, :], rcmp[:, 1, i, :, :], tie, ALU.mult))
                    link(V.tensor_tensor(rcmp[:, 0, i, :, :], rcmp[:, 0, i, :, :], rcmp[:, 2, i, :, :], ALU.add))
                link(V.tensor_reduce(rwork[:, 3, :, :], rcmp[:, 0, :, :, :], AX.X, ALU.add))
                link(V.tensor_reduce(rmax[:, 0, :], lg[:], AX.X, ALU.max))
                V.tensor_scalar(sel[:, :, 0:EXPERTS], rwork[:, 3, :, :], 1.5, None, ALU.is_lt).then_inc(s_sel, 1)
                for i in range(NT):
                    V.tensor_scalar(rwork[:, 0, i, :], lg[:, i, :], rmax[:, 0, i:i + 1], None, ALU.subtract)\
                        .then_inc(s_m1, 1)
                for i in range(NT):
                    dve.wait_ge(s_xb, i + 1)
                    V.tensor_tensor(xn[:, i, :], xn[:, i, :], xb[0][:, i, :], ALU.subtract).then_inc(s_xr, 1)
                dve.wait_ge(s_sel, 1)
                dve.wait_ge(s_rexp, 1)
                link(V.tensor_tensor(rwork[:, 2, :, :], rwork[:, 1, :, :], sel[:, :, 0:EXPERTS], ALU.mult))
                link(V.tensor_reduce(rmax[:, 1, :], rwork[:, 2, :, :], AX.X, ALU.add))
                link(V.reciprocal(rmax[:, 0, :], rmax[:, 1, :]))
                link(V.tensor_tensor(gate[:, :, 0:EXPERTS], rwork[:, 2, :, :], spread(rmax[:, 0, :], 2, EXPERTS),
                                     ALU.mult))
                dve.wait_ge(s_rankp, 1)
                n = EXPERTS
                V.tensor_copy(rank[:], ps[:, 1, 0:2 * n].rearrange("p (i e) -> p i e", i=NT))
                link(V.tensor_reduce(cmx[:], ps[:, 1, 2 * n:2 * n + EXPERTS], AX.X, ALU.max))
                V.tensor_scalar(over[:], cmx[:], P + 0.5, None, ALU.is_gt).then_inc(s_over, 1)
                for i in range(NT):
                    dve.wait_ge(s_xb, NT + i + 1)
                    V.tensor_tensor(xb[2][:, i, :], xn[:, i, :], xb[1][:, i, :], ALU.subtract).then_inc(s_xb2, 1)
                dve.wait_ge(s_over, 1)

            def picks(rnd, e):
                slots = const("slot").rearrange("p (r s) -> p r s", r=NT)[:, rnd, :]
                for i in range(NT):
                    last = V.tensor_scalar(pick[:, i, :], slots, rank[:, i, bass.ds(e, 1)], sel[:, i, bass.ds(e, 1)],
                                           ALU.is_equal, ALU.mult)
                last.then_inc(s_pick, 1)

            def picked(n):
                for half in range(2):
                    dve.wait_ge(s_xeh, 2 * n + (half + 1))
                    for q in range(4):
                        c = 4 * half + q
                        last = V.scalar_tensor_tensor(
                            out=hTl[:, c, 0:P], in0=ps[:, 6 + half, q * P:(q + 1) * P],
                            scalar=param(1, "ln_ffn")[:, c:c + 1], in1=hTh[:, c, 0:P].bitcast(F32),
                            op0=ALU.mult, op1=ALU.subtract)
                    last.then_inc(s_xel, 1)

            def expert(e, rnd, follows):
                ex = e + rnd * EXPERTS
                ue = NT * STEPS + ex * STEPS
                qe = PASS + ex * PASS

                def next_pick():
                    dve.wait_ge(s_spt, ex + 1)
                    picks(rnd, e + 1)

                steps(1, ue, qe, next_pick if follows else None)
                turned(1, ue, STEPS - 1)
                if follows:
                    ups(qe + PASS, 0, range(UP // 2))
                    picked(ex + 1)
                    ups(qe + PASS, 0, range(UP // 2, UP))
                for n in range(2):
                    dve.wait_ge(s_yeh, 2 * ex + (n + 1))
                    V.tensor_tensor(yel[:, n, :], ps[:, 4 + n, :], yeh[:, n, :].bitcast(F32), ALU.subtract)\
                        .then_inc(s_yel, 1)
                if follows:
                    ups(qe + PASS, 1, range(UP // 2))
                for n in range(2):
                    for i in range(NT):
                        dve.wait_ge(s_scat, 4 * ex + (2 * n + i + 1))
                        xs = x[:, i, n * 512:(n + 1) * 512]
                        V.scalar_tensor_tensor(out=xs, in0=ps[:, SCATTER[i][n], :], scalar=gate[:, i, bass.ds(e, 1)],
                                               in1=xs, op0=ALU.mult, op1=ALU.add).then_inc(s_xadd, 1)

            def experts(rnd):
                first = rnd * EXPERTS
                if rnd:
                    dve.wait_ge(s_spt, first)
                picks(rnd, 0)
                if rnd:
                    ups(PASS + first * PASS, 0, range(UP))
                picked(first)
                ups(PASS + first * PASS, 1, range(UP // 2))
                with dve.Fori(0, EXPERTS - 1) as e:
                    expert(e, rnd, True)
                expert(EXPERTS - 1, rnd, False)
                dve.wait_ge(s_xadd, 4 * EXPERTS * (rnd + 1) + 1)

            dve.nop().then_inc(s_xadd, 1)
            V.memset(hc[:], 0.0)
            link(V.memset(blocks[:], 0.0))
            mixer(0)
            dense()
            mixer(1)
            routing()
            experts(0)
            more = dve.value_load(over[0:1, 0:1], min_val=0, max_val=1)
            with dve.If(more > 0):
                experts(1)
            dve.nop().then_inc(s_last, 1)
            rms_apply(2 * DEPTH, gain=gfin[:])

        @block.gpsimd
        def _(pool):
            pass


def _constants():
    c = np.zeros((P, CONST_COLS), np.float32)

    def put(name, v):
        a, n = CONSTS[name]
        c[:, a:a + n] = np.asarray(v, np.float32).reshape(P, n)

    p = np.arange(P)
    put("ident", np.eye(P))
    put("causal", np.where(p[None, :] <= p[:, None], 0.0, NEG))
    tok = p[:, None, None] + P * np.arange(NT)[None, :, None]
    blk = np.arange(CB)[None, None, :]
    seen = (blk * CMP_STRIDE + CMP_LEN - 1 <= tok) & (blk < NBLK)
    put("cmp_add", np.where(seen, 0.0, NEG))
    put("cmp_keep", seen)
    put("head_block", p[:, None] // CB == np.arange(HEADS)[None, :])
    half = HD // 2
    inv = np.float32(10000.0) ** (-np.arange(half, dtype=np.float32) / np.float32(half))
    ang = (tok.astype(np.float32) * inv[None, None, :]).astype(np.float32)
    put("cos", np.concatenate([np.cos(ang), np.cos(ang)], -1))
    put("sin", np.concatenate([-np.sin(ang), np.sin(ang)], -1))
    lg = np.log1p(-np.exp2(-5.0 - np.arange(RET_HEADS)))
    rel = np.arange(T)[None, None, :] - p[:, None, None]
    put("decay", np.where(rel >= 0, np.exp(np.maximum(rel, 0) * lg[None, :, None]) * SCALE, 0.0))
    put("before", p[:, None] < p[None, :])
    put("ones", np.ones((P, P)))
    put("slot", np.broadcast_to(np.arange(NT * P)[None, :], (P, NT * P)))
    e = np.arange(EXPERTS)
    put("earlier", np.broadcast_to((e[None, :] < e[:, None])[None], (P, EXPERTS, EXPERTS)))
    return c


def _by_partition(w, k):
    return w.reshape(k, P, -1).transpose(1, 0, 2)


def _layout(a):
    f = {n: np.asarray(v) for n, v in a.items()}
    q = [np.r_[c * HD:(c + 1) * HD, (4 + c) * HD:(5 + c) * HD] for c in range(HPG)]
    at = lambda s, n: np.arange(s, s + n)
    kc, vc, ks, vs, kw, vw = (at(512 + n * 128, 128) for n in range(6))
    gl, conv = at(1280, 24), at(1304, 512)
    rq, rk, rv, rg = (at(1816 + n * 256, 256) for n in range(4))
    cols = [np.concatenate(q + [ks, kw]), np.concatenate([kc, vc, conv]), np.concatenate([vs, vw, gl, rk]),
            np.concatenate([rq, rv, rg])]
    mix, params = [], []
    for l in range(DEPTH):
        parts = [_by_partition(f["w_in"][l][:, c], KD) for c in cols]
        w1 = [_by_partition(f["cmp_w1"][l, v], 16) for v in range(2)]
        w2 = [_by_partition(f["cmp_w2"][l, v], 2) for v in range(2)]
        pw = _by_partition(f["conv_pw"][l], NC)
        flat = lambda *z: np.concatenate([y.reshape(P, -1) for y in z], axis=1)
        parts.append(flat(w1[0], np.concatenate([w2[0], w2[0]], axis=2)))
        parts.append(flat(w1[1], w2[1], pw))
        wo = _by_partition(f["w_out"][l], KD)
        parts += [wo[:, :, :512], wo[:, :, 512:]]
        mix.append(np.concatenate([np.ascontiguousarray(z).reshape(-1) for z in parts]))
        wide = lambda v: v.reshape(-1, P).T
        pe = f["cmp_pe"][l].reshape(2, 16, P).transpose(2, 0, 1).reshape(P, 32)
        cw = f["conv_w"][l].T.reshape(NC, P, CONV_K).transpose(1, 0, 2).reshape(P, -1)
        params.append(np.concatenate([
            wide(f["ln_attn"][l]), wide(f["ln_ffn"][l]), pe, cw, wide(f["conv_b"][l]), wide(f["conv_ln_g"][l]),
            wide(f["conv_ln_b"][l]), np.broadcast_to(f["ret_gn"][l][None], (P, RET_HEADS * HD))], axis=1))

    def ffn(w13, w2):
        n = w13.shape[0]
        up = w13.reshape(n, KD, P, 2, STEPS, FC).transpose(0, 4, 2, 1, 3, 5).reshape(n, STEPS, P, -1)
        down = w2.reshape(n, STEPS, FC // P, P, D).transpose(0, 1, 3, 2, 4).reshape(n, STEPS, P, -1)
        return np.concatenate([up, down], axis=3).reshape(n * STEPS, P, FFN_ITEM)

    c = np.ascontiguousarray
    return {
        "x_in": c(f["x"].reshape(T, D)), "consts_in": _constants(), "params_in": c(np.stack(params, axis=1)),
        "mix_in": c(np.stack(mix)), "ffn_in": ffn(f["ffn_w13"], f["ffn_w2"]), "moe_in": ffn(f["moe_w13"][0], f["moe_w2"][0]),
        "router_in": c(_by_partition(f["router"][0], KD)), "final_in": c(np.broadcast_to(f["ln_final"][None], (P, D))),
    }


_ORDER = ["x_in", "consts_in", "params_in", "mix_in", "ffn_in", "moe_in", "router_in", "final_in"]


def kernel(**inputs):
    import concourse.bacc as _bacc
    from concourse.bass_utils import run_bass_kernel_spmd as _run

    nc = _bacc.Bacc("TRN2", target_bir_lowering=False, num_devices=1)
    arrays = _layout(inputs)
    args = [nc.dram_tensor(n, arrays[n].shape, F32, kind="ExternalInput").ap() for n in _ORDER]
    args.append(nc.dram_tensor("out_0", (T, D), F32, kind="ExternalOutput").ap())
    hybrid_trunk_kernel(nc, *args)
    r = _run(nc, [arrays], core_ids=[0])
    return r.results[0]["out_0"].reshape(1, T, D)
```
